# Optimizing a Trainium2 kernel written in Bass

```python
import math
import jax, jax.numpy as jnp
from jax import lax
import numpy as np

D_MODEL = 1024
BATCH = 1
SEQ = 4096
DEPTH = 1

CHUNK = 64
MIX_WIDTH = D_MODEL
POOL_WIDTH = MIX_WIDTH // 2
ATTN_WIDTH = MIX_WIDTH - POOL_WIDTH
POOL_WINDOWS = (2, 4, 8, 16)
N_POOL_GROUPS = len(POOL_WINDOWS)
POOL_GROUP_DIM = POOL_WIDTH // N_POOL_GROUPS
HEAD_DIM = 64
N_HEADS = ATTN_WIDTH // HEAD_DIM
LEFT_CHUNKS = 8
BAND = (LEFT_CHUNKS + 1) * CHUNK
MAX_REL = 64
N_REL = 2 * MAX_REL + 1
IN_PROJ_WIDTH = 2 * POOL_WIDTH + 4 * ATTN_WIDTH
EPS = 1e-6
MASK_VALUE = -1e30

kernel_name = "hybrid_pool_chunkattn_block"

def rms_norm(x, g):
    xf = x.astype(jnp.float32)
    y = xf * lax.rsqrt(jnp.mean(xf * xf, axis=-1, keepdims=True) + EPS)
    return (y * g.astype(jnp.float32)).astype(x.dtype)

def multiscale_pool(v, pool_w, pool_scale):
    S = v.shape[1]
    vf = v.astype(jnp.float32)
    cs = jnp.pad(jnp.cumsum(vf, axis=1), ((0, 0), (1, 0), (0, 0)))
    t = jnp.arange(S)
    diffs = []
    for gi, w in enumerate(POOL_WINDOWS):
        sl = slice(gi * POOL_GROUP_DIM, (gi + 1) * POOL_GROUP_DIM)
        cs_g = cs[..., sl]
        lo = jnp.maximum(t + 1 - w, 0)
        win_sum = cs_g[:, 1:] - jnp.take(cs_g, lo, axis=1)
        count = (t + 1 - lo).astype(jnp.float32)[None, :, None]
        diffs.append(win_sum / count - vf[..., sl])
    d = jnp.stack(diffs, axis=2)
    y = jnp.einsum('bsgc,gcd->bsgd', d, pool_w.astype(jnp.float32))
    y = y.reshape(y.shape[0], S, POOL_WIDTH) * pool_scale.astype(jnp.float32)
    return y.astype(v.dtype)

def chunked_rel_attention(q, k, v, rel_bias):
    B, S, H, Dh = q.shape
    n_chunks = S // CHUNK
    pad = LEFT_CHUNKS * CHUNK
    kp = jnp.pad(k, ((0, 0), (pad, 0), (0, 0), (0, 0)))
    vp = jnp.pad(v, ((0, 0), (pad, 0), (0, 0), (0, 0)))
    qc = jnp.moveaxis(q.reshape(B, n_chunks, CHUNK, H, Dh), 1, 0)
    i = jnp.arange(CHUNK)
    j = jnp.arange(BAND)
    rel = j[None, :] - pad - i[:, None]
    rel_idx = jnp.clip(rel, -MAX_REL, MAX_REL) + MAX_REL
    bias = rel_bias.astype(jnp.float32)[:, rel_idx]
    scale = 1.0 / math.sqrt(Dh)

    def one_chunk(args):
        c, qb = args
        start = c * CHUNK
        kb = lax.dynamic_slice_in_dim(kp, start, BAND, axis=1)
        vb = lax.dynamic_slice_in_dim(vp, start, BAND, axis=1)
        s = jnp.einsum('bqhd,bkhd->bhqk', qb, kb).astype(jnp.float32) * scale + bias[None]
        valid = (start + j - pad) >= 0
        s = jnp.where(valid[None, None, None, :], s, MASK_VALUE)
        p = jax.nn.softmax(s, axis=-1)
        return jnp.einsum('bhqk,bkhd->bqhd', p.astype(vb.dtype), vb)

    out = lax.map(one_chunk, (jnp.arange(n_chunks), qc))
    return jnp.moveaxis(out, 0, 1).reshape(B, S, H * Dh)

def setup_inputs(seed: int = 0) -> dict:
    key = jax.random.key(seed)
    ks = jax.random.split(key, 9)
    x = jax.random.normal(ks[0], (BATCH, SEQ, D_MODEL), jnp.float32)
    norm_gain = 1.0 + 0.02 * jax.random.normal(ks[1], (DEPTH, D_MODEL), jnp.float32)
    w_in = jax.random.normal(ks[2], (DEPTH, D_MODEL, IN_PROJ_WIDTH), jnp.float32) * D_MODEL ** -0.5
    pool_w = jax.random.normal(ks[3], (DEPTH, N_POOL_GROUPS, POOL_GROUP_DIM, POOL_GROUP_DIM), jnp.float32) * POOL_GROUP_DIM ** -0.5
    pool_scale = 1.0 + 0.02 * jax.random.normal(ks[4], (DEPTH, POOL_WIDTH), jnp.float32)
    rel_bias = 0.5 * jax.random.normal(ks[5], (DEPTH, N_HEADS, N_REL), jnp.float32)
    w_out = jax.random.normal(ks[6], (DEPTH, MIX_WIDTH, D_MODEL), jnp.float32) * MIX_WIDTH ** -0.5
    final_norm_gain = 1.0 + 0.02 * jax.random.normal(ks[7], (D_MODEL,), jnp.float32)
    return {"x": x, "norm_gain": norm_gain, "w_in": w_in, "pool_w": pool_w,
            "pool_scale": pool_scale, "rel_bias": rel_bias, "w_out": w_out,
            "final_norm_gain": final_norm_gain}

def reference(x, norm_gain, w_in, pool_w, pool_scale, rel_bias, w_out, final_norm_gain):
    B, S, _ = x.shape
    for layer in range(DEPTH):
        h = rms_norm(x, norm_gain[layer])
        proj = jnp.einsum('bsd,de->bse', h, w_in[layer])
        o = 0
        pool_v = proj[..., o:o + POOL_WIDTH]; o += POOL_WIDTH
        pool_g = proj[..., o:o + POOL_WIDTH]; o += POOL_WIDTH
        q = proj[..., o:o + ATTN_WIDTH]; o += ATTN_WIDTH
        k = proj[..., o:o + ATTN_WIDTH]; o += ATTN_WIDTH
        v = proj[..., o:o + ATTN_WIDTH]; o += ATTN_WIDTH
        attn_g = proj[..., o:o + ATTN_WIDTH]
        y_pool = multiscale_pool(pool_v, pool_w[layer], pool_scale[layer]) * jax.nn.silu(pool_g)
        qh = q.reshape(B, S, N_HEADS, HEAD_DIM)
        kh = k.reshape(B, S, N_HEADS, HEAD_DIM)
        vh = v.reshape(B, S, N_HEADS, HEAD_DIM)
        y_attn = chunked_rel_attention(qh, kh, vh, rel_bias[layer]) * jax.nn.silu(attn_g)
        y = jnp.concatenate([y_pool, y_attn], axis=-1)
        x = x + jnp.einsum('bse,ed->bsd', y, w_out[layer])
    return rms_norm(x, final_norm_gain)


_drawn_inputs = setup_inputs


def setup_inputs(seed=0):
    import zlib

    import numpy as np

    out = dict(_drawn_inputs(seed))
    spreads = {}
    factors = {'norm_gain': 5.269, 'pool_scale': 8.0, 'rel_bias': 4.543, 'final_norm_gain': 2.862}
    for name, (base, spread) in spreads.items():
        noise = np.random.default_rng([zlib.crc32(name.encode()), seed]).standard_normal(out[name].shape)
        drawn = base * np.exp(spread * noise) if base else spread * noise
        out[name] = __import__('jax').numpy.asarray(drawn.astype(out[name].dtype))
    for name, factor in factors.items():
        out[name] = (out[name] * factor).astype(out[name].dtype)
    return out
```

```python
import math
from contextlib import ExitStack

import concourse.bass as bass
from concourse import mybir

F32 = mybir.dt.float32
F16 = mybir.dt.float16
BF16 = mybir.dt.bfloat16
ALU = mybir.AluOpType
ACT = mybir.ActivationFunctionType

P = 128
SEQ, D = 4096, 1024
KT = D // P
POOL, ATTN, DH, HEADS = 512, 512, 64, 8
WINDOWS = (2, 4, 8, 16)
GROUPS = len(WINDOWS)
CHUNK, MAX_REL = 64, 64
N_REL = 2 * MAX_REL + 1
EPS = 1e-6
NEG = -1e30

WS = 64.0
YS = 1.0 / 16
PS = 16.0

PT = 512
PTILES = SEQ // PT
PBLK = PT // P
HIST = 16
GORDER = (3, 2, 1, 0)

AT = 256
ATILES = SEQ // AT
RING = 6
NKT = ATTN // P
CHUNKS_LOOPED = 2
GROUP_BLOCKS = (((0, 0, 1), (1, 0, 2), (5, 1, 1)), ((2, 0, 2), (3, 0, 2)), ((4, 0, 2),))
GROUP_AT = (0, 512, 1024)
GROUP_BIAS = ((384, 128, 0), (256, 128, 128), (0, 256, 0))
EXT = 2 * P + 512


def at_least(eng, sem, n):
    if not isinstance(n, int) or n > 0:
        eng.wait_ge(sem, n)


def place(i, j):
    for g, blocks in enumerate(GROUP_BLOCKS):
        c = GROUP_AT[g]
        for bi, j0, n in blocks:
            if bi == i and j0 <= j < j0 + n:
                return c + (j - j0) * P
            c += n * P
    raise ValueError


def build(nc, x, norm_gain, w_in, pool_w, pool_scale, rel_fwd, rel_rev, w_out, final_gain, out):
    x_blk = x.rearrange("a (n p) d -> (a n) p d", p=P)
    out_blk = out.rearrange("a (n p) d -> (a n) p d", p=P)
    win_v = w_in[0].rearrange("(k p) n -> p k n", p=P)
    wout_v = w_out[0].rearrange("(k p) n -> k p n", p=P)
    h_dram = nc.dram_tensor("h_split", (ATILES, P, 2 * KT * AT), F16, kind="Internal").ap()
    r_dram = nc.dram_tensor("residual", (SEQ // P, P, D), F32, kind="Internal").ap()
    rel_dram = nc.dram_tensor("rel_rows", (2, HEADS, EXT), F32, kind="Internal").ap()
    bq_dram = nc.dram_tensor("bias_by_query", (HEADS, P, 640), F32, kind="Internal").ap()
    bk_dram = nc.dram_tensor("bias_by_key", (HEADS, P, 256), F32, kind="Internal").ap()

    ctx = ExitStack()
    with ctx:
        def sb(stack, name, shape, dt):
            return stack.enter_context(nc.sbuf_tensor(name, shape, dt))

        def sem(name):
            return ctx.enter_context(nc.semaphore(name))

        psum = [ctx.enter_context(nc.psum_tensor(f"bank{i}", [P, 512], F32)) for i in range(6)]
        wide = ctx.enter_context(nc.psum_tensor("bank67", [P, 1024], F32))

        ident = sb(ctx, "ident", [P, P], F32)
        ident16 = sb(ctx, "ident16", [P, P], F16)
        wa_h = sb(ctx, "wa_h", [P, 16, KT * P], F16)
        wa_l = sb(ctx, "wa_l", [P, 16, KT * P], F16)
        wob_h = sb(ctx, "wob_h", [P, NKT, D], F16)
        wob_l = sb(ctx, "wob_l", [P, NKT, D], F16)
        stat = sb(ctx, "stat", [P, 16], F32)
        pow_half = sb(ctx, "pow_half", [P, 1], F32)
        eps = sb(ctx, "eps", [P, 1], F32)

        pctx = ExitStack()
        wp_h = sb(pctx, "wp_h", [P, 8, KT * P], F16)
        wp_l = sb(pctx, "wp_l", [P, 8, KT * P], F16)
        wot_h = sb(pctx, "wot_h", [P, NKT, D], F16)
        wot_l = sb(pctx, "wot_l", [P, NKT, D], F16)
        wst = sb(pctx, "wst", [P, 2, KT, P], F32)
        xin = sb(pctx, "xin", [P, 2, D], F32)
        xn = sb(pctx, "xn", [P, D], F32)
        xres = sb(pctx, "xres", [P, 2, D], F32)
        gain = sb(pctx, "gain", [P, D], F32)
        junk = sb(pctx, "junk", [P, D], BF16)
        hT = sb(pctx, "hT", [P, 2, KT, PT], F16)
        vb = sb(pctx, "vb", [P, 2, HIST + PT], F32)
        win = sb(pctx, "win", [P, 2, HIST + PT], F32)
        carry = sb(pctx, "carry", [P, GROUPS, HIST], F32)
        sig = sb(pctx, "sig", [P, PT], F32)
        yp_h = sb(pctx, "yp_h", [P, 2, NKT, PT], F16)
        yp_l = sb(pctx, "yp_l", [P, 2, NKT, PT], F16)
        inv_count = sb(pctx, "inv_count", [P, GROUPS, HIST], F32)
        psc = sb(pctx, "psc", [P, GROUPS], F32)
        rel = sb(pctx, "rel", [HEADS, 2, N_REL], F32)
        pw = vb[:, 0, 0:PT].rearrange("p (g e) -> p g e", g=GROUPS)
        wvT = xres[:, 1, :]
        ext = yp_l[0:HEADS, :, :, :].rearrange("p a k n -> p (a k n)").bitcast(F32)[:, 0:2 * EXT].rearrange(
            "p (r u) -> p r u", r=2)

        names = """ident0 ident_ready id16 consts small_loaded ext_done ext_stored bias_stored psc_done
            w_hi w_lo fold_t fold_copied fold_mm
            ss_done ms_done rstd_done xn_done tr_done xth_done xtl_done h_stored
            v_mm g_mm vb_done sig_done z_done step_done y_done yh_done yl_done op_mm r_done
            phase_done""".split()
        S = {n: sem("p_" + n) for n in names}
        w_loaded = [sem(f"p_w_loaded{s}") for s in range(2)]
        x_loaded = [sem(f"p_x_loaded{s}") for s in range(2)]
        xres_loaded = [sem(f"p_xres_loaded{s}") for s in range(2)]
        r_stored = [sem(f"p_r_stored{s}") for s in range(2)]

        chunks = []
        for g in GORDER:
            chunks += [("v", g), ("g", g)]
        chunks += [("top", k) for k in range(NKT)] + [("bottom", k) for k in range(NKT)]
        STARTUP = len(chunks)

        def steps_before(t, k):
            done = sum(3 + g + 1 for g in GORDER[:k])
            total = sum(3 + g + 1 for g in GORDER)
            if isinstance(t, int) and t == 0:
                return done + 2 * k
            return total * t + 2 * GROUPS + done

        pj = psum[0:4]
        tr = psum[4:6]
        op = [wide[:, 0:512], wide[:, 512:1024]]

        def p_phase_pe(pe):
            def fold(k, g):
                n = 2 * k
                pe.wait_ge(w_loaded[0], 16 * (n // 2 + 1))
                if k == 0:
                    pe.wait_ge(S["ident_ready"], 1)
                    pe.wait_ge(S["small_loaded"], 16 * 5)
                at_least(pe, S["fold_copied"], 2 * k)
                for half in range(2):
                    for q in range(4):
                        mm = nc.tensor.transpose(tr[half][:, q * P:(q + 1) * P], wst[:, 0, 4 * half + q, :], ident[:, :])
                    mm.then_inc(S["fold_t"], 1)
                pe.wait_ge(S["fold_copied"], 2 * k + 2)
                at_least(pe, S["w_lo"], n - 1)
                for half in range(2):
                    for q in range(4):
                        c = 4 * half + q
                        mm = nc.tensor.matmul(pj[half][:, q * P:(q + 1) * P], wvT[:, c * P:(c + 1) * P],
                                              pw[:, g, :], start=True, stop=True)
                    mm.then_inc(S["fold_mm"], 1)

            def transposes(t, b):
                n = PBLK * t + b
                pe.wait_ge(S["xn_done"], n + 1)
                for half in range(2):
                    if isinstance(n, int):
                        at_least(pe, S["xtl_done"], 2 * (n - 1) + half + 1)
                        if n == 0:
                            pe.wait_ge(S["fold_copied"], 2 * GROUPS)
                    else:
                        pe.wait_ge(S["xtl_done"], 2 * (n - 1) + half + 1)
                    for q in range(4):
                        c = 4 * half + q
                        mm = nc.tensor.transpose(tr[half][:, q * P:(q + 1) * P], xn[:, c * P:(c + 1) * P], ident[:, :])
                    mm.then_inc(S["tr_done"], 1)

            def project(t):
                pe.wait_ge(S["xtl_done"], 2 * PBLK * t + 2 * PBLK)
                for k, g in enumerate(GORDER):
                    for what in range(2):
                        bank = pj[(2 * k + what) % 4]
                        if isinstance(t, int) and t == 0 and k < 2:
                            pe.wait_ge(S["w_lo"], 2 * GROUPS)
                        elif what == 0:
                            pe.wait_ge(S["vb_done"], GROUPS * t + k - 1)
                        else:
                            pe.wait_ge(S["z_done"], GROUPS * t + k - 1)
                        c = 4 * what + g
                        for kt in range(KT):
                            wh = wp_h[:, c, kt * P:(kt + 1) * P]
                            wl = wp_l[:, c, kt * P:(kt + 1) * P]
                            nc.tensor.matmul(bank[:, :], wh, hT[:, 0, kt, :], start=(kt == 0), stop=False)
                            nc.tensor.matmul(bank[:, :], wh, hT[:, 1, kt, :], start=False, stop=False)
                            mm = nc.tensor.matmul(bank[:, :], wl, hT[:, 0, kt, :], start=False, stop=(kt == KT - 1))
                        mm.then_inc(S["g_mm" if what else "v_mm"], 1)

            def output(t, ts, b):
                n = PBLK * t + b
                if b == 0:
                    pe.wait_ge(S["yl_done"], GROUPS * t + GROUPS)
                    if ts == 0:
                        pe.wait_ge(S["w_lo"], 2 * GROUPS + NKT)
                if b > 0 or (isinstance(t, int) and t == PTILES - 1):
                    pe.wait_ge(S["r_done"], 2 * n)
                for kt in range(NKT):
                    yh = yp_h[:, ts % 2, kt, b * P:(b + 1) * P]
                    yl = yp_l[:, ts % 2, kt, b * P:(b + 1) * P]
                    for part, w in ((yh, wot_h), (yh, wot_l), (yl, wot_h)):
                        for n2 in range(2):
                            mm = nc.tensor.matmul(op[n2], part, w[:, kt, n2 * 512:(n2 + 1) * 512],
                                                  start=(kt == 0 and w is wot_h and part is yh),
                                                  stop=(kt == NKT - 1 and part is yl))
                mm.then_inc(S["op_mm"], 1)

            for k, g in enumerate(GORDER):
                fold(k, g)
            for b in range(PBLK):
                transposes(0, b)
            project(0)
            for b in range(PBLK):
                transposes(1, b)
            with pe.Fori(0, (PTILES - 2) // 2) as it:
                for u in range(2):
                    t = 2 * it + (1 + u)
                    project(t)
                    for b in range(PBLK):
                        transposes(t + 1, b)
                        output(t - 1, u, b)
            last = PTILES - 1
            project(last)
            for t in (last - 1, last):
                for b in range(PBLK):
                    output(t, t, b)

        def p_phase_act(act):
            def split_hi(n):
                kind, c = chunks[n]
                s = n % 2
                if kind == "v":
                    k = n // 2
                    for half in range(2):
                        act.wait_ge(S["fold_t"], 2 * k + half + 1)
                        if k:
                            act.wait_ge(S["fold_mm"], 2 * k)
                        nc.scalar.activation(wvT[:, half * 512:(half + 1) * 512], tr[half][:, :],
                                             ACT.Copy).then_inc(S["fold_copied"], 1)
                    for half in range(2):
                        act.wait_ge(S["fold_mm"], 2 * k + half + 1)
                        ins = nc.scalar.activation(wp_h[:, c, half * 512:(half + 1) * 512], pj[half][:, :],
                                                   ACT.Copy, scale=WS)
                    ins.then_inc(S["w_hi"], 1)
                    return
                act.wait_ge(w_loaded[s], 16 * (n // 2 + 1))
                dst = {"g": lambda: wp_h[:, 4 + c, :], "top": lambda: wot_h[:, c, :],
                       "bottom": lambda: wob_h[:, c, :]}[kind]()
                nc.scalar.activation(dst, wst[:, s, :, :].rearrange("p k n -> p (k n)"), ACT.Copy,
                                     scale=WS).then_inc(S["w_hi"], 1)

            def split_hi_looped(t, i):
                act.wait_ge(w_loaded[i], 8 * STARTUP + 16 * t + 16)
                nc.scalar.activation(wa_h[:, CHUNKS_LOOPED * t + i, :], wst[:, i, :, :].rearrange("p k n -> p (k n)"),
                                     ACT.Copy, scale=WS).then_inc(S["w_hi"], 1)

            def square(t, b):
                n = PBLK * t + b
                act.wait_ge(x_loaded[b % 2], 16 * (2 * t + b // 2 + 1))
                if isinstance(n, int):
                    at_least(act, S["ms_done"], n - 1)
                    at_least(act, S["ss_done"], n)
                else:
                    act.wait_ge(S["ms_done"], n - 1)
                    act.wait_ge(S["ss_done"], n)
                nc.scalar.activation(junk[:, :], xin[:, b % 2, :], ACT.Square, scale=D ** -0.5,
                                     accum_out=stat[:, b % 2:b % 2 + 1]).then_inc(S["ss_done"], 1)

            def h_hi(t, b):
                for half in range(2):
                    act.wait_ge(S["tr_done"], 2 * (PBLK * t + b) + half + 1)
                    if b == 0 and half == 0 and not (isinstance(t, int) and t == 0):
                        act.wait_ge(S["g_mm"], GROUPS * t)
                        act.wait_ge(S["h_stored"], 32 * t)
                    nc.scalar.activation(hT[:, 0, 4 * half:4 * half + 4, b * P:(b + 1) * P],
                                         tr[half][:, :].rearrange("p (k n) -> p k n", k=4),
                                         ACT.Copy).then_inc(S["xth_done"], 1)

            def value(t, k):
                m = GROUPS * t + k
                act.wait_ge(S["v_mm"], m + 1)
                if isinstance(m, int):
                    at_least(act, S["yl_done"], m - 1)
                    if m == 0:
                        act.wait_ge(S["fold_mm"], 2 * GROUPS)
                else:
                    act.wait_ge(S["yl_done"], m - 1)
                nc.scalar.activation(vb[:, k % 2, HIST:], pj[(2 * k) % 4][:, :], ACT.Copy,
                                     scale=1 / WS).then_inc(S["vb_done"], 1)
                act.wait_ge(S["g_mm"], m + 1)
                if not (isinstance(m, int) and m == 0):
                    act.wait_ge(S["y_done"], m)
                nc.scalar.activation(sig[:, :], pj[(2 * k + 1) % 4][:, :], ACT.Tanh,
                                     scale=0.5 / WS).then_inc(S["sig_done"], 1)

            def y_hi(t, ts, k):
                m = GROUPS * t + k
                act.wait_ge(S["y_done"], m + 1)
                nc.scalar.activation(yp_h[:, ts % 2, GORDER[k], :], vb[:, k % 2, HIST:],
                                     ACT.Copy).then_inc(S["yh_done"], 1)

            def tile(t, ts, more=True):
                value(t, 0)
                if more:
                    square(t + 1, 0)
                    square(t + 1, 1)
                value(t, 1)
                y_hi(t, ts, 0)
                split_hi_looped(t, 0)
                value(t, 2)
                y_hi(t, ts, 1)
                if more:
                    square(t + 1, 2)
                split_hi_looped(t, 1)
                value(t, 3)
                y_hi(t, ts, 2)
                y_hi(t, ts, 3)
                if more:
                    for b in range(PBLK):
                        h_hi(t + 1, b)
                        if b == 0:
                            square(t + 1, 3)

            square(0, 0)
            square(0, 1)
            act.wait_ge(S["small_loaded"], 16 * 5)
            nc.scalar.activation(psc[:, :], psc[:, :], ACT.Copy, scale=YS * 0.5 / WS).then_inc(S["psc_done"], 1)
            for n in range(2 * GROUPS):
                split_hi(n)
            square(0, 2)
            for b in range(PBLK):
                h_hi(0, b)
                if b == 0:
                    square(0, 3)
            for n in range(2 * GROUPS, STARTUP):
                split_hi(n)
            tile(0, 0)
            with act.Fori(0, (PTILES - 2) // 2) as it:
                for u in range(2):
                    tile(2 * it + (1 + u), 1 + u)
            tile(PTILES - 1, PTILES - 1, more=False)

        def p_phase_dve(dve):
            def split_lo(n):
                kind, c = chunks[n]
                s = n % 2
                dve.wait_ge(S["w_hi"], n + 1)
                if kind == "v":
                    for half in range(2):
                        cols = slice(half * 512, (half + 1) * 512)
                        ins = nc.vector.scalar_tensor_tensor(
                            out=wp_l[:, c, cols], in0=pj[half][:, :], scalar=WS, in1=wp_h[:, c, cols],
                            op0=ALU.mult, op1=ALU.subtract)
                    ins.then_inc(S["w_lo"], 1)
                    return
                hi, lo = {"g": (wp_h, wp_l), "top": (wot_h, wot_l), "bottom": (wob_h, wob_l)}[kind]
                i = 4 + c if kind == "g" else c
                nc.vector.scalar_tensor_tensor(
                    out=lo[:, i, :], in0=wst[:, s, :, :].rearrange("p k n -> p (k n)"), scalar=WS,
                    in1=hi[:, i, :], op0=ALU.mult, op1=ALU.subtract).then_inc(S["w_lo"], 1)

            def split_lo_looped(t, i):
                c = CHUNKS_LOOPED * t + i
                dve.wait_ge(S["w_hi"], STARTUP + 1 + c)
                nc.vector.scalar_tensor_tensor(
                    out=wa_l[:, c, :], in0=wst[:, i, :, :].rearrange("p k n -> p (k n)"), scalar=WS,
                    in1=wa_h[:, c, :], op0=ALU.mult, op1=ALU.subtract).then_inc(S["w_lo"], 1)

            def normalise(t, b):
                n = PBLK * t + b
                dve.wait_ge(S["rstd_done"], n + 1)
                if isinstance(n, int):
                    if n == 0:
                        dve.wait_ge(S["small_loaded"], 16 * 5)
                    at_least(dve, S["tr_done"], 2 * n)
                else:
                    dve.wait_ge(S["tr_done"], 2 * n)
                nc.vector.scalar_tensor_tensor(
                    out=xn[:, :], in0=xin[:, b % 2, :], scalar=stat[:, 4 + b % 2:5 + b % 2],
                    in1=gain[:, :], op0=ALU.mult, op1=ALU.mult).then_inc(S["xn_done"], 1)

            def h_lo(t, b):
                for half in range(2):
                    dve.wait_ge(S["xth_done"], 2 * (PBLK * t + b) + half + 1)
                    nc.vector.tensor_tensor(
                        hT[:, 1, 4 * half:4 * half + 4, b * P:(b + 1) * P],
                        tr[half][:, :].rearrange("p (k n) -> p k n", k=4),
                        hT[:, 0, 4 * half:4 * half + 4, b * P:(b + 1) * P],
                        ALU.subtract).then_inc(S["xtl_done"], 1)

            def pool(t, k):
                g = GORDER[k]
                w = WINDOWS[g]
                m = GROUPS * t + k
                first = isinstance(t, int) and t == 0
                step = [steps_before(t, k)]

                def link(ins):
                    ins.then_inc(S["step_done"], 1)
                    step[0] = step[0] + 1
                    return step[0]

                v = vb[:, k % 2, :]
                dve.wait_ge(S["sig_done"], m + 1)
                nc.vector.scalar_tensor_tensor(
                    out=sig[:, :], in0=sig[:, :], scalar=1.0, in1=pj[(2 * k + 1) % 4][:, :],
                    op0=ALU.add, op1=ALU.mult).then_inc(S["z_done"], 1)
                if first:
                    link(nc.vector.memset(v[:, 0:HIST], 0.0))
                else:
                    dve.wait_ge(S["step_done"], step[0])
                    link(nc.vector.tensor_copy(v[:, 0:HIST], carry[:, g, :]))
                dve.wait_ge(S["step_done"], step[0])
                dve.wait_ge(S["vb_done"], m + 1)
                link(nc.vector.tensor_copy(carry[:, g, :], v[:, PT:PT + HIST]))
                src, back = v, 1
                for level in range(g + 1):
                    dst = win[:, level % 2, :]
                    lo = 2 * back - 1
                    dve.wait_ge(S["step_done"], step[0])
                    link(nc.vector.tensor_tensor(dst[:, lo:], src[:, lo:], src[:, lo - back:HIST + PT - back], ALU.add))
                    src, back = dst, 2 * back
                other = win[:, (g + 1) % 2, 0:PT]
                dve.wait_ge(S["step_done"], step[0])
                link(nc.vector.scalar_tensor_tensor(
                    out=other, in0=src[:, HIST:], scalar=1.0 / w, in1=v[:, HIST:], op0=ALU.mult, op1=ALU.subtract))
                if first:
                    dve.wait_ge(S["step_done"], step[0])
                    dve.wait_ge(S["consts"], 3)
                    link(nc.vector.tensor_tensor(src[:, HIST:2 * HIST], src[:, HIST:2 * HIST], inv_count[:, g, :], ALU.mult))
                    dve.wait_ge(S["step_done"], step[0])
                    link(nc.vector.tensor_tensor(other[:, 0:HIST], src[:, HIST:2 * HIST], v[:, HIST:2 * HIST], ALU.subtract))
                dve.wait_ge(S["step_done"], step[0])
                dve.wait_ge(S["z_done"], m + 1)
                if first and k == 0:
                    dve.wait_ge(S["psc_done"], 1)
                nc.vector.scalar_tensor_tensor(
                    out=v[:, HIST:], in0=other, scalar=psc[:, g:g + 1], in1=sig[:, :],
                    op0=ALU.mult, op1=ALU.mult).then_inc(S["y_done"], 1)

            def residual(t, b):
                n = PBLK * t + b
                dve.wait_ge(S["op_mm"], n + 1)
                dve.wait_ge(xres_loaded[b % 2], 16 * (2 * t + b // 2 + 1))
                for n2 in range(2):
                    cols = slice(n2 * 512, (n2 + 1) * 512)
                    nc.vector.scalar_tensor_tensor(
                        out=xres[:, b % 2, cols], in0=op[n2], scalar=1.0 / (WS * YS), in1=xres[:, b % 2, cols],
                        op0=ALU.mult, op1=ALU.add).then_inc(S["r_done"], 1)

            def tile(t, more=True, before=True):
                pool(t, 0)
                if more:
                    normalise(t + 1, 0)
                pool(t, 1)
                split_lo_looped(t, 0)
                pool(t, 2)
                split_lo_looped(t, 1)
                pool(t, 3)
                for b in range(PBLK):
                    if more:
                        h_lo(t + 1, b)
                        if b + 1 < PBLK:
                            normalise(t + 1, b + 1)
                    if before:
                        residual(t - 1, b)

            dve.wait_ge(S["ident_ready"], 1)
            nc.vector.tensor_copy(ident16[:, :], ident[:, :]).then_inc(S["id16"], 1)
            dve.wait_ge(S["small_loaded"], 16 * 5)
            for r in range(2):
                below = EXT - P - MAX_REL - 1 if r == 0 else P - MAX_REL - 1
                far = rel[:, r, 0:1] if r == 0 else rel[:, r, N_REL - 1:N_REL]
                above = EXT - below - N_REL
                for cols, src in ((slice(0, below), rel[:, r, 0:1].to_broadcast([HEADS, below])),
                                  (slice(below, below + N_REL), rel[:, r, :]),
                                  (slice(below + N_REL, EXT), rel[:, r, N_REL - 1:N_REL].to_broadcast([HEADS, above]))):
                    nc.vector.tensor_scalar(ext[:, r, cols], src, far, None, ALU.subtract).then_inc(S["ext_done"], 1)
            for n in range(2 * GROUPS):
                split_lo(n)
            for b in range(PBLK):
                normalise(0, b)
                h_lo(0, b)
            for n in range(2 * GROUPS, STARTUP):
                split_lo(n)
            tile(0, before=False)
            with dve.Fori(0, PTILES - 2) as it:
                tile(it + 1)
            tile(PTILES - 1, more=False)
            for b in range(PBLK):
                residual(PTILES - 1, b)

        def p_phase_pool(pool):
            def rstd(t, b):
                n = PBLK * t + b
                s = b % 2
                pool.wait_ge(S["ss_done"], n + 1)
                if isinstance(n, int):
                    at_least(pool, S["xn_done"], n - 1)
                else:
                    pool.wait_ge(S["xn_done"], n - 1)
                nc.gpsimd.tensor_tensor(stat[:, 2 + s:3 + s], stat[:, s:s + 1], eps[:, :], ALU.add).then_inc(S["ms_done"], 1)
                pool.wait_ge(S["ms_done"], n + 1)
                nc.gpsimd.tensor_tensor(stat[:, 4 + s:5 + s], stat[:, 2 + s:3 + s], pow_half[:, :],
                                        ALU.pow).then_inc(S["rstd_done"], 1)

            def y_lo(t, ts, k):
                m = GROUPS * t + k
                pool.wait_ge(S["yh_done"], m + 1)
                if ts == 0 and k == 0:
                    pool.wait_ge(S["ext_stored"], 16)
                nc.gpsimd.tensor_tensor(yp_l[:, ts % 2, GORDER[k], :], vb[:, k % 2, HIST:],
                                        yp_h[:, ts % 2, GORDER[k], :], ALU.subtract).then_inc(S["yl_done"], 1)

            def tile(t, ts, more=True):
                if more:
                    rstd(t + 1, 0)
                    rstd(t + 1, 1)
                y_lo(t, ts, 0)
                y_lo(t, ts, 1)
                if more:
                    rstd(t + 1, 2)
                y_lo(t, ts, 2)
                y_lo(t, ts, 3)
                if more:
                    rstd(t + 1, 3)

            nc.gpsimd.memset(ident[:, :], 0.0).then_inc(S["ident0"], 1)
            pool.wait_ge(S["ident0"], 1)
            nc.gpsimd.affine_select(out=ident[:, :], in_=ident[:, :], compare_op=ALU.not_equal, fill=1.0,
                                    base=0, pattern=[[-1, P]], channel_multiplier=1).then_inc(S["ident_ready"], 1)
            nc.gpsimd.memset(pow_half[:, :], -0.5).then_inc(S["consts"], 1)
            nc.gpsimd.memset(eps[:, :], EPS).then_inc(S["consts"], 1)
            pool.wait_ge(S["consts"], 2)
            for b in range(3):
                rstd(0, b)
            for g, w in enumerate(WINDOWS):
                for c in range(w - 1):
                    nc.gpsimd.memset(inv_count[:, g, c:c + 1], 1.0 / (c + 1))
                ins = nc.gpsimd.memset(inv_count[:, g, w - 1:], 1.0 / w)
            ins.then_inc(S["consts"], 1)
            rstd(0, 3)
            tile(0, 0)
            with pool.Fori(0, (PTILES - 2) // 2) as it:
                for u in range(2):
                    tile(2 * it + (1 + u), 1 + u)
            tile(PTILES - 1, PTILES - 1, more=False)

        def p_phase_sp(sp):
            def load_chunk(n):
                kind, c = chunks[n]
                if n >= 2:
                    sp.wait_ge(S["w_lo"], n - 1)
                src = wout_v[c if kind == "top" else NKT + c] if kind in ("top", "bottom") else \
                    win_v[:, :, (c + (0 if kind == "v" else GROUPS)) * P:(c + 1 + (0 if kind == "v" else GROUPS)) * P]
                dst = wst[:, n % 2, :, :]
                if kind in ("top", "bottom"):
                    dst = dst.rearrange("p k n -> p (k n)")
                sp.dma_start(dst, src).then_inc(w_loaded[n % 2], 16)

            def load_chunk_looped(t, i):
                c = CHUNKS_LOOPED * t + i
                sp.wait_ge(S["w_lo"], STARTUP + c - 1)
                start = (c + 2 * GROUPS) * P
                src = win_v[:, :, bass.ds(start, P)]
                sp.dma_start(wst[:, i, :, :], src).then_inc(w_loaded[i], 16)

            def load_x(t, b):
                n = PBLK * t + b
                if isinstance(n, int):
                    at_least(sp, S["xn_done"], n - 1)
                else:
                    sp.wait_ge(S["xn_done"], n - 1)
                sp.dma_start(xin[:, b % 2, :], x_blk[n]).then_inc(x_loaded[b % 2], 16)

            def load_res(t, b):
                n = PBLK * t + b
                if isinstance(n, int) and n < 2:
                    if n == 1:
                        sp.wait_ge(S["fold_mm"], 2 * GROUPS)
                else:
                    sp.wait_ge(r_stored[b % 2], 16 * (2 * t + b // 2))
                sp.dma_start(xres[:, b % 2, :], x_blk[n]).then_inc(xres_loaded[b % 2], 16)

            def store_res(t, b):
                n = PBLK * t + b
                sp.wait_ge(S["r_done"], 2 * n + 2)
                sp.dma_start(r_dram[n], xres[:, b % 2, :]).then_inc(r_stored[b % 2], 16)

            def store_h(t):
                sp.wait_ge(S["xtl_done"], 2 * PBLK * t + 2 * PBLK)
                for half in range(2):
                    sp.dma_start(h_dram[2 * t + half].rearrange("p (a n) -> p a n", a=2 * KT),
                                 hT[:, :, :, half * AT:(half + 1) * AT].rearrange("p s k n -> p (s k) n")
                                 ).then_inc(S["h_stored"], 16)

            def stores(t, more=True):
                for b in range(PBLK):
                    store_res(t, b)
                    if more or b < 2:
                        load_res(t if b < 2 else t + 1, (b + 2) % PBLK)

            def tile(t, more=True, before=True):
                if more:
                    load_x(t + 1, 0)
                    load_x(t + 1, 1)
                for i in range(CHUNKS_LOOPED):
                    load_chunk_looped(t, i)
                if more:
                    load_x(t + 1, 2)
                    load_x(t + 1, 3)
                if before:
                    stores(t - 1)
                if more:
                    store_h(t + 1)

            load_x(0, 0)
            for g in range(1):
                load_chunk(0)
            sp.dma_start(pw[:, :, :], pool_w[0].rearrange("g c e -> c g e")).then_inc(S["small_loaded"], 16)
            sp.dma_start(gain[:, :], norm_gain[0:1, :].to_broadcast([P, D])).then_inc(S["small_loaded"], 16)
            load_chunk(1)
            load_x(0, 1)
            sp.dma_start(psc[:, :], pool_scale[0].rearrange("(g p) -> p g", p=P),
                         allow_slow_non_contiguous=True).then_inc(S["small_loaded"], 16)
            sp.dma_start(rel[:, 0, :], rel_fwd).then_inc(S["small_loaded"], 16)
            sp.dma_start(rel[:, 1, :], rel_rev).then_inc(S["small_loaded"], 16)
            sp.dma_start(xres[:, 0, :], x_blk[0]).then_inc(xres_loaded[0], 16)
            for n in range(2, 2 * GROUPS):
                load_chunk(n)
            load_res(0, 1)
            load_x(0, 2)
            load_x(0, 3)
            sp.wait_ge(S["ext_done"], 6)
            sp.dma_start(rel_dram.rearrange("r h u -> h r u"), ext[:, :, :]).then_inc(S["ext_stored"], 16)
            for n in range(2 * GROUPS, STARTUP):
                load_chunk(n)
            store_h(0)
            sp.wait_ge(S["ext_stored"], 16)
            for r, (dst, width) in enumerate(((bq_dram, 640), (bk_dram, 256))):
                sp.dma_start(dst, bass.AP(rel_dram.tensor, r * HEADS * EXT + P - 1, [[EXT, HEADS], [-1, P], [1, width]])
                             ).then_inc(S["bias_stored"], 16)
            tile(0, before=False)
            with sp.Fori(0, PTILES - 2) as it:
                tile(it + 1)
            tile(PTILES - 1, more=False)
            stores(PTILES - 1, more=False)
            sp.wait_ge(S["bias_stored"], 32)
            sp.wait_ge(S["h_stored"], 32 * PTILES)
            for s in range(2):
                sp.wait_ge(r_stored[s], 16 * 2 * PTILES)

        pctx.close()

        actx = ctx
        hT2 = sb(actx, "hT2", [P, 2, KT, AT], F16)
        nat = sb(actx, "nat", [P, 2, 2, 4, AT], F16)
        qs = sb(actx, "qs", [P, HEADS, AT], F16)
        qm = sb(actx, "qm", [DH + 1, HEADS, AT], F16)
        ks = sb(actx, "ks", [P, HEADS, RING * P], F16)
        kl = sb(actx, "kl", [DH + 1, HEADS, RING * P], F16)
        v_h = sb(actx, "v_h", [P, RING, HEADS, DH + 1], F16)
        v_l = sb(actx, "v_l", [P, RING, HEADS, DH], F16)
        sig2 = sb(actx, "sig2", [P, ATTN], F32)
        gate = sb(actx, "gate", [P, 2, ATTN], F32)
        p32 = sb(actx, "p32", [P, 2, 512], F32)
        p_h = sb(actx, "p_h", [P, 2, 1280], F16)
        p_l = sb(actx, "p_l", [P, 2, 1280], F16)
        bias_q = sb(actx, "bias_q", [P, HEADS, 640], BF16)
        bias_k = sb(actx, "bias_k", [P, HEADS, 256], F32)
        junk2 = sb(actx, "junk2", [P, 640], BF16)
        mx = sb(actx, "mx", [P, 2, 2], F32)
        m16 = sb(actx, "m16", [P, 2, 2], F16)
        rc = sb(actx, "rc", [P, 2, 2], F32)
        y = sb(actx, "y", [P, 2, ATTN], F32)
        yT_h = sb(actx, "yT_h", [P, NKT, AT], F16)
        yT_l = sb(actx, "yT_l", [P, NKT, AT], F16)
        res = sb(actx, "res", [P, 2, D], F32)
        fgain = sb(actx, "fgain", [P, D], F32)
        edge = sb(actx, "edge", [1, P + CHUNK], BF16)

        names = """phase v_ones k_ones edge bias_q_loaded bias_k_loaded mask_done fg_loaded h_loaded
            proj_mm proj_hi proj_lo moved_k moved_q
            max_mm max_begun max_done m16_done mrow_mm mrow_done st_mm bias_done exp_done ph_done pl_done
            pv_mm rc_done ya_done yt_mm yth_done ytl_done op_mm res_done ss_done ms_done rstd_done fin_done""".split()
        A = {n: sem("a_" + n) for n in names}
        res_loaded = [sem(f"a_res_loaded{s}") for s in range(2)]
        out_stored = [sem(f"a_out_stored{s}") for s in range(2)]

        pja = psum[0:2]
        sta = psum[2:4]
        pva = psum[4]
        tra = psum[5]
        UNITS = 12
        KSCALE, QSCALE = 1 / WS, 1 / (WS * math.sqrt(DH))
        YSCALE = YS * 0.5 / WS

        def ring(ts, i):
            return (2 * ts - 4 + i) % RING

        def first_block(ts):
            return max(0, 4 - 2 * ts)

        def groups(ts):
            found = []
            for g, blocks in enumerate(GROUP_BLOCKS):
                have = [b for b in blocks if b[0] >= first_block(ts)]
                if have:
                    found.append((g, have))
            return found

        def seq(t, ts, h, k):
            n = len(groups(ts))
            if ts == 0:
                return n * h + k
            return HEADS * 3 * t - HEADS + n * h + k

        def span(g, have):
            cols = [(place(i, j0) - GROUP_AT[g], n * P) for i, j0, n in have]
            return cols[0][0], cols[-1][0] + cols[-1][1]

        def a_tiles(eng, tile):
            tile(0, 0)
            tile(1, 1)
            looped = (ATILES - 2) // 3
            with eng.Fori(0, looped) as it:
                for u in range(3):
                    tile(3 * it + (2 + u), 2 + u)
            for t in range(2 + 3 * looped, ATILES):
                tile(t, t)

        def a_phase_pe(pe):
            def project(t, ts):
                pe.wait_ge(A["h_loaded"], 16 * t + 16)
                for u in range(UNITS):
                    bank = pja[u % 2]
                    if u < 2:
                        if ts >= 2:
                            pe.wait_ge(A["res_done"], 4 * (t - 1))
                        elif ts == 1:
                            pe.wait_ge(A["proj_lo"], UNITS)
                    else:
                        pe.wait_ge(A["proj_lo"], UNITS * t + u - 1)
                    if u < 8:
                        c = (u + 4) % 8
                        for kt in range(KT):
                            wh = wa_h[:, c, kt * P:(kt + 1) * P]
                            wl = wa_l[:, c, kt * P:(kt + 1) * P]
                            nc.tensor.matmul(bank[:, 0:AT], wh, hT2[:, 0, kt, :], start=(kt == 0), stop=False)
                            nc.tensor.matmul(bank[:, 0:AT], wh, hT2[:, 1, kt, :], start=False, stop=False)
                            mm = nc.tensor.matmul(bank[:, 0:AT], wl, hT2[:, 0, kt, :], start=False, stop=(kt == KT - 1))
                    else:
                        j, c = (u - 8) // 2, 8 + 4 * (u % 2)
                        for kt in range(KT):
                            hh = hT2[:, 0, kt, j * P:(j + 1) * P]
                            hl = hT2[:, 1, kt, j * P:(j + 1) * P]
                            wh = wa_h[:, c:c + 4, kt * P:(kt + 1) * P]
                            wl = wa_l[:, c:c + 4, kt * P:(kt + 1) * P]
                            dst = bank[:, :].rearrange("p (c n) -> p c n", c=4)
                            nc.tensor.matmul(dst, hh, wh, start=(kt == 0), stop=False)
                            nc.tensor.matmul(dst, hh, wl, start=False, stop=False)
                            mm = nc.tensor.matmul(dst, hl, wh, start=False, stop=(kt == KT - 1))
                    mm.then_inc(A["proj_mm"], 1)

            def maxima(t, ts, h, j):
                if h == 0 and j == 0:
                    pe.wait_ge(A["moved_k"], 96 * t + 96)
                    pe.wait_ge(A["moved_q"], 96 * t + 96)
                n = 2 * HEADS * t + 2 * h + j
                if not (ts == 0 and h == 0 and j == 0):
                    pe.wait_ge(A["max_done"], n)
                if ts > 0 and h == 0 and j == 0:
                    pe.wait_ge(A["ytl_done"], 2 * t)
                c = max(0, first_block(ts) - j) * P
                while c < 640:
                    i = j + c // P
                    run = 1
                    while (c + run * P < 640 and (c + run * P) % 512 and ring(ts, i + run) == ring(ts, i) + run):
                        run += 1
                    r = ring(ts, i)
                    mm = nc.tensor.matmul(wide[:, c:c + run * P], qs[0:DH, h, j * P:(j + 1) * P],
                                          ks[0:DH, h, r * P:(r + run) * P], start=True, stop=True)
                    c += run * P
                mm.then_inc(A["max_mm"], 1)

            def max_rows(t, ts, h):
                pe.wait_ge(A["m16_done"], HEADS * t + h + 1)
                if not (ts == 0 and h == 0):
                    pe.wait_ge(A["mrow_done"], HEADS * t + h)
                if h == 0 and ts > 0:
                    pe.wait_ge(A["ytl_done"], 2 * t)
                for j in range(2):
                    mm = nc.tensor.matmul(tra[DH:DH + 1, j * P:(j + 1) * P], m16[:, h % 2, j:j + 1], ident16[:, :],
                                          start=True, stop=True)
                mm.then_inc(A["mrow_mm"], 1)

            def scores(t, ts, h, k):
                g, have = groups(ts)[k]
                n = seq(t, ts, h, k)
                bank = sta[seq(ts, ts, h, k) % 2]
                if not (isinstance(n, int) and n < 2):
                    pe.wait_ge(A["exp_done"], n - 1)
                if k == 0:
                    pe.wait_ge(A["mrow_done"], HEADS * t + h + 1)
                for i, j0, w in have:
                    r = ring(ts, i)
                    c = place(i, j0) - GROUP_AT[g]
                    dst = bank[:, c:c + w * P]
                    qcols = slice(j0 * P, (j0 + w) * P)
                    masked = i < 2
                    nc.tensor.matmul(dst, ks[:, h, r * P:(r + 1) * P], qs[:, h, qcols], start=True, stop=False)
                    mm = nc.tensor.matmul(dst, kl[:, h, r * P:(r + 1) * P], qm[:, h, qcols], start=False, stop=not masked)
                    if masked:
                        m0 = c + (i - j0) * P + CHUNK
                        mm = nc.tensor.matmul(bank[:, m0:m0 + CHUNK], edge[:, 0:P], edge[:, P:P + CHUNK],
                                              start=False, stop=True)
                mm.then_inc(A["st_mm"], 1)

            def values(t, ts, h):
                n = seq(t, ts, h, len(groups(ts)))
                pe.wait_ge(A["pl_done"], n)
                if not (ts == 0 and h == 0):
                    pe.wait_ge(A["ya_done"], 2 * (HEADS * t + h))
                for j in range(2):
                    blocks = [i for i in range(j, j + 5) if i >= first_block(ts)]
                    acc = pva[:, j * (DH + 1):(j + 1) * (DH + 1)]
                    for i in blocks:
                        c, r = place(i, j), ring(ts, i)
                        ph, pl = p_h[:, h % 2, c:c + P], p_l[:, h % 2, c:c + P]
                        nc.tensor.matmul(acc, ph, v_h[:, r, h, :], start=(i == blocks[0]), stop=False)
                        nc.tensor.matmul(acc[:, 0:DH], ph, v_l[:, r, h, :], start=False, stop=False)
                        mm = nc.tensor.matmul(acc, pl, v_h[:, r, h, :], start=False, stop=(i == blocks[-1]))
                mm.then_inc(A["pv_mm"], 1)

            def branch_transposes(t, ts):
                for j in range(2):
                    bank = tra if j == 0 else wide
                    pe.wait_ge(A["ya_done"], 2 * HEADS * t + 2 * HEADS)
                    for q in range(NKT):
                        mm = nc.tensor.transpose(bank[:, q * P:(q + 1) * P], y[:, j, q * P:(q + 1) * P], ident[:, :])
                    mm.then_inc(A["yt_mm"], 1)

            def output(t, ts, h):
                j, kt = h // 4, h % 4
                if h == 0:
                    pe.wait_ge(A["ytl_done"], 2 * t + 2)
                if kt == 0:
                    if j == 0 and ts == ATILES - 1:
                        pe.wait_ge(A["res_done"], 4 * t)
                    elif j == 0:
                        pe.wait_ge(A["proj_lo"], UNITS * t + 2 * UNITS)
                    else:
                        pe.wait_ge(A["res_done"], 4 * t + 2)
                yh, yl = yT_h[:, kt, j * P:(j + 1) * P], yT_l[:, kt, j * P:(j + 1) * P]
                for part, w in ((yh, wob_h), (yh, wob_l), (yl, wob_h)):
                    for n2 in range(2):
                        mm = nc.tensor.matmul(pja[n2][:, :], part, w[:, kt, n2 * 512:(n2 + 1) * 512],
                                              start=(kt == 0 and part is yh and w is wob_h),
                                              stop=(kt == NKT - 1 and part is yl))
                if kt == NKT - 1:
                    mm.then_inc(A["op_mm"], 1)

            def tile(t, ts):
                project(t, ts)
                if ts > 0:
                    branch_transposes(t - 1, ts - 1)
                for j in range(2):
                    maxima(t, ts, 0, j)
                max_rows(t, ts, 0)
                for h in range(HEADS):
                    for k in range(len(groups(ts))):
                        scores(t, ts, h, k)
                        if k < 2 and h + 1 < HEADS:
                            maxima(t, ts, h + 1, k)
                    if ts > 0:
                        output(t - 1, ts - 1, h)
                    if h > 0:
                        values(t, ts, h - 1)
                    if h + 1 < HEADS:
                        max_rows(t, ts, h + 1)
                values(t, ts, HEADS - 1)

            pe.wait_ge(A["phase"], 5)
            pe.wait_ge(A["edge"], 3)
            pe.wait_ge(A["v_ones"], 1)
            pe.wait_ge(A["k_ones"], 1)
            a_tiles(pe, tile)
            branch_transposes(ATILES - 1, ATILES - 1)
            for h in range(HEADS):
                output(ATILES - 1, ATILES - 1, h)

        def a_phase_act(act):
            def project_hi(t, ts):
                for u in range(UNITS):
                    m = UNITS * t + u
                    act.wait_ge(A["proj_mm"], m + 1)
                    bank = pja[u % 2]
                    if u < 8:
                        which, pair = u // 4, u % 4
                        if pair == 0 and ts > 0:
                            act.wait_ge(A["moved_q" if which else "moved_k"], 96 * t)
                        ins = nc.scalar.activation(nat[:, which, 0, pair, :], bank[:, 0:AT], ACT.Copy,
                                                   scale=QSCALE if which else KSCALE)
                    else:
                        j = (u - 8) // 2
                        if u % 2 == 0:
                            r = ring(ts, 4 + j)
                            ins = nc.scalar.activation(v_h[:, r, :, 0:DH], bank[:, :].rearrange("p (h d) -> p h d", h=HEADS),
                                                       ACT.Copy, scale=1 / WS)
                        else:
                            act.wait_ge(A["proj_lo"], m - 1)
                            if u == 9 and ts >= 2:
                                act.wait_ge(A["ss_done"], 2 * (t - 1))
                            ins = nc.scalar.activation(sig2[:, :], bank[:, :], ACT.Tanh, scale=0.5 / WS)
                    ins.then_inc(A["proj_hi"], 1)

            def branch_hi(t):
                for j in range(2):
                    bank = tra if j == 0 else wide
                    act.wait_ge(A["yt_mm"], 2 * t + j + 1)
                    nc.scalar.activation(yT_h[:, :, j * P:(j + 1) * P],
                                         bank[:, 0:512].rearrange("p (k n) -> p k n", k=NKT),
                                         ACT.Copy, scale=YSCALE).then_inc(A["yth_done"], 1)

            def max_row(t, ts, h):
                act.wait_ge(A["mrow_mm"], HEADS * t + h + 1)
                nc.scalar.activation(qm[DH:DH + 1, h, :], tra[DH:DH + 1, 0:AT], ACT.Copy).then_inc(A["mrow_done"], 1)

            def exponentials(t, ts, h):
                for k, (g, have) in enumerate(groups(ts)):
                    n = seq(t, ts, h, k)
                    s = seq(ts, ts, h, k) % 2
                    a, b = span(g, have)
                    act.wait_ge(A["bias_done"], n + 1)
                    if not (isinstance(n, int) and n < 2):
                        act.wait_ge(A["pl_done"], n - 1)
                    nc.scalar.activation(p32[:, s, a:b], sta[s][:, a:b], ACT.Exp).then_inc(A["exp_done"], 1)
                    act.wait_ge(A["exp_done"], n + 1)
                    if k == 0 and not (ts == 0 and h < 2):
                        act.wait_ge(A["pv_mm"], HEADS * t + h - 1)
                    c = GROUP_AT[g]
                    nc.scalar.activation(p_h[:, h % 2, c + a:c + b], p32[:, s, a:b], ACT.Copy).then_inc(A["ph_done"], 1)

            def square(t, ts, j):
                n = 2 * t + j
                act.wait_ge(A["res_done"], 2 * n + 2)
                if not (ts == 0 and j == 0):
                    act.wait_ge(A["ss_done"], n)
                if ts > 0:
                    act.wait_ge(A["ms_done"], n - 1)
                nc.scalar.activation(sig2[:, :].bitcast(BF16), res[:, j, :], ACT.Square, scale=D ** -0.5,
                                     accum_out=stat[:, 8 + j:9 + j]).then_inc(A["ss_done"], 1)

            def tile(t, ts):
                project_hi(t, ts)
                if ts > 0:
                    branch_hi(t - 1)
                max_row(t, ts, 0)
                for h in range(HEADS):
                    exponentials(t, ts, h)
                    if h + 1 < HEADS:
                        max_row(t, ts, h + 1)
                    if h == 5 and ts > 0:
                        square(t - 1, ts - 1, 0)
                if ts > 0:
                    square(t - 1, ts - 1, 1)

            act.wait_ge(A["phase"], 5)
            a_tiles(act, tile)
            branch_hi(ATILES - 1)
            for j in range(2):
                square(ATILES - 1, ATILES - 1, j)

        def a_phase_dve(dve):
            def project_lo(t, ts):
                for u in range(UNITS):
                    m = UNITS * t + u
                    dve.wait_ge(A["proj_hi"], m + 1)
                    bank = pja[u % 2]
                    if u < 8:
                        which, pair = u // 4, u % 4
                        ins = nc.vector.scalar_tensor_tensor(
                            out=nat[:, which, 1, pair, :], in0=bank[:, 0:AT], scalar=QSCALE if which else KSCALE,
                            in1=nat[:, which, 0, pair, :], op0=ALU.mult, op1=ALU.subtract)
                    else:
                        j = (u - 8) // 2
                        if u % 2 == 0:
                            r = ring(ts, 4 + j)
                            ins = nc.vector.scalar_tensor_tensor(
                                out=v_l[:, r, :, :], in0=bank[:, :].rearrange("p (h d) -> p h d", h=HEADS), scalar=1 / WS,
                                in1=v_h[:, r, :, 0:DH], op0=ALU.mult, op1=ALU.subtract)
                        else:
                            ins = nc.vector.scalar_tensor_tensor(
                                out=gate[:, j, :], in0=sig2[:, :], scalar=1.0, in1=bank[:, :],
                                op0=ALU.add, op1=ALU.mult)
                    ins.then_inc(A["proj_lo"], 1)

            def branch_lo(t):
                for j in range(2):
                    bank = tra if j == 0 else wide
                    dve.wait_ge(A["yth_done"], 2 * t + j + 1)
                    nc.vector.scalar_tensor_tensor(
                        out=yT_l[:, :, j * P:(j + 1) * P], in0=bank[:, 0:512].rearrange("p (k n) -> p k n", k=NKT),
                        scalar=YSCALE, in1=yT_h[:, :, j * P:(j + 1) * P],
                        op0=ALU.mult, op1=ALU.subtract).then_inc(A["ytl_done"], 1)

            def maximum(t, ts, h, j):
                n = 2 * HEADS * t + 2 * h + j
                c = max(0, first_block(ts) - j) * P
                dve.wait_ge(A["max_mm"], n + 1)
                if not (ts == 0 and h == 0 and j == 0):
                    dve.wait_ge(A["max_done"], n)
                if j == 0 and not (ts == 0 and h < 2):
                    dve.wait_ge(A["m16_done"], HEADS * t + h - 1)
                dve.sem_inc(A["max_begun"], 1)
                nc.vector.tensor_tensor_reduce(
                    junk2[:, c:640], wide[:, c:640], bias_q[:, h, c:640], 1.0, -3e38, ALU.add, ALU.max,
                    mx[:, h % 2, j:j + 1]).then_inc(A["max_done"], 1)

            def minus_max(t, ts, h):
                dve.wait_ge(A["max_done"], 2 * (HEADS * t + h + 1))
                if not (ts == 0 and h < 2):
                    dve.wait_ge(A["mrow_mm"], HEADS * t + h - 1)
                nc.vector.tensor_scalar(m16[:, h % 2, :], mx[:, h % 2, :], -1.0, math.log(PS),
                                        ALU.mult, ALU.add).then_inc(A["m16_done"], 1)

            def add_bias(t, ts, h, k):
                g, have = groups(ts)[k]
                n = seq(t, ts, h, k)
                bank = sta[seq(ts, ts, h, k) % 2]
                c, w, b = GROUP_BIAS[g]
                dve.wait_ge(A["st_mm"], n + 1)
                nc.vector.tensor_tensor(bank[:, c:c + w], bank[:, c:c + w], bias_k[:, h, b:b + w],
                                        ALU.add).then_inc(A["bias_done"], 1)

            def attend(t, ts, h):
                n = HEADS * t + h
                acc = pva[:, 0:2 * (DH + 1)].rearrange("p (j d) -> p j d", j=2)
                dve.wait_ge(A["pv_mm"], n + 1)
                if not (ts == 0 and h < 2):
                    dve.wait_ge(A["ya_done"], 2 * (n - 1))
                nc.vector.reciprocal(rc[:, h % 2, :], acc[:, :, DH]).then_inc(A["rc_done"], 1)
                dve.wait_ge(A["rc_done"], n + 1)
                if h == 0 and ts > 0:
                    dve.wait_ge(A["yt_mm"], 2 * t)
                for j in range(2):
                    nc.vector.scalar_tensor_tensor(
                        out=y[:, j, h * DH:(h + 1) * DH], in0=acc[:, j, 0:DH], scalar=rc[:, h % 2, j:j + 1],
                        in1=gate[:, j, h * DH:(h + 1) * DH], op0=ALU.mult, op1=ALU.mult).then_inc(A["ya_done"], 1)

            def residual(t, j):
                n = 2 * t + j
                dve.wait_ge(A["op_mm"], n + 1)
                dve.wait_ge(res_loaded[j], 16 * t + 16)
                for n2 in range(2):
                    cols = slice(n2 * 512, (n2 + 1) * 512)
                    nc.vector.scalar_tensor_tensor(
                        out=res[:, j, cols], in0=pja[n2][:, :], scalar=1.0 / (WS * YS), in1=res[:, j, cols],
                        op0=ALU.mult, op1=ALU.add).then_inc(A["res_done"], 1)

            def finish(t, j):
                n = 2 * t + j
                dve.wait_ge(A["rstd_done"], n + 1)
                nc.vector.scalar_tensor_tensor(
                    out=res[:, j, :], in0=res[:, j, :], scalar=stat[:, 12 + j:13 + j], in1=fgain[:, :],
                    op0=ALU.mult, op1=ALU.mult).then_inc(A["fin_done"], 1)

            def tile(t, ts):
                project_lo(t, ts)
                if ts > 0:
                    branch_lo(t - 1)
                for j in range(2):
                    maximum(t, ts, 0, j)
                minus_max(t, ts, 0)
                for h in range(HEADS):
                    for k in range(len(groups(ts))):
                        add_bias(t, ts, h, k)
                        if k < 2 and h + 1 < HEADS:
                            maximum(t, ts, h + 1, k)
                    if h + 1 < HEADS:
                        minus_max(t, ts, h + 1)
                    if h > 0:
                        attend(t, ts, h - 1)
                    if ts > 0 and h == 3:
                        residual(t - 1, 0)
                    if ts > 0 and h == 6:
                        finish(t - 1, 0)
                attend(t, ts, HEADS - 1)
                if ts > 0:
                    residual(t - 1, 1)
                    finish(t - 1, 1)

            dve.wait_ge(A["phase"], 5)
            nc.vector.memset(v_h[:, :, :, DH:DH + 1], 1.0).then_inc(A["v_ones"], 1)
            dve.wait_ge(A["bias_q_loaded"], 16)
            dve.wait_ge(A["bias_k_loaded"], 16)
            dve.wait_ge(A["fg_loaded"], 16)
            nc.vector.memset(bias_q[CHUNK:P, :, 0:CHUNK], NEG).then_inc(A["mask_done"], 1)
            nc.vector.memset(bias_q[0:CHUNK, :, 640 - CHUNK:640], NEG).then_inc(A["mask_done"], 1)
            nc.vector.memset(bias_k[CHUNK:P, :, 0:CHUNK], NEG).then_inc(A["mask_done"], 1)
            dve.wait_ge(A["mask_done"], 3)
            a_tiles(dve, tile)
            branch_lo(ATILES - 1)
            for j in range(2):
                residual(ATILES - 1, j)
            for j in range(2):
                finish(ATILES - 1, j)

        def a_phase_pool(pool):
            def p_lo(t, ts, h):
                for k, (g, have) in enumerate(groups(ts)):
                    n = seq(t, ts, h, k)
                    s = seq(ts, ts, h, k) % 2
                    a, b = span(g, have)
                    c = GROUP_AT[g]
                    pool.wait_ge(A["ph_done"], n + 1)
                    nc.gpsimd.tensor_tensor(p_l[:, h % 2, c + a:c + b], p32[:, s, a:b], p_h[:, h % 2, c + a:c + b],
                                            ALU.subtract).then_inc(A["pl_done"], 1)

            def rstd(t, ts, j):
                n = 2 * t + j
                pool.wait_ge(A["ss_done"], n + 1)
                if ts > 0:
                    pool.wait_ge(A["fin_done"], n - 1)
                nc.gpsimd.tensor_tensor(stat[:, 10 + j:11 + j], stat[:, 8 + j:9 + j], eps[:, :], ALU.add).then_inc(A["ms_done"], 1)
                pool.wait_ge(A["ms_done"], n + 1)
                nc.gpsimd.tensor_tensor(stat[:, 12 + j:13 + j], stat[:, 10 + j:11 + j], pow_half[:, :],
                                        ALU.pow).then_inc(A["rstd_done"], 1)

            def tile(t, ts):
                for h in range(HEADS):
                    p_lo(t, ts, h)
                    if ts > 0 and h == 5:
                        rstd(t - 1, ts - 1, 0)
                if ts > 0:
                    rstd(t - 1, ts - 1, 1)

            pool.wait_ge(A["phase"], 5)
            nc.gpsimd.memset(kl[DH:DH + 1, :, :], 1.0).then_inc(A["k_ones"], 1)
            nc.gpsimd.memset(edge[:, 0:CHUNK], NEG).then_inc(A["edge"], 1)
            nc.gpsimd.memset(edge[:, CHUNK:P], 0.0).then_inc(A["edge"], 1)
            nc.gpsimd.memset(edge[:, P:], 1.0).then_inc(A["edge"], 1)
            pool.dma_start(bias_q[:, :, :], bq_dram.rearrange("h p c -> p h c")).then_inc(A["bias_q_loaded"], 16)
            a_tiles(pool, tile)
            for j in range(2):
                rstd(ATILES - 1, ATILES - 1, j)

        def a_phase_sp(sp):
            def load_h(t):
                sp.dma_start(hT2[:, :, :, :].rearrange("p s k n -> p (s k n)"), h_dram[t]).then_inc(A["h_loaded"], 16)

            def move(dst, src, name):
                sp.dma_start(dst, src).then_inc(A[name], 16)

            def tile(t, ts):
                if ts > 0:
                    for j in range(2):
                        if ts > 1:
                            sp.wait_ge(out_stored[j], 16 * (t - 1))
                        sp.dma_start(res[:, j, :], r_dram[2 * (t - 1) + j]).then_inc(res_loaded[j], 16)
                r = ring(ts, 4) * P
                new = slice(r, r + AT)
                sp.wait_ge(A["proj_lo"], UNITS * t + 4)
                for o in range(2):
                    half = slice(o * DH, (o + 1) * DH)
                    for p0 in (0, DH):
                        move(ks[p0:p0 + DH, o::2, new], nat[half, 0, 0, :, :], "moved_k")
                    move(kl[0:DH, o::2, new], nat[half, 0, 1, :, :], "moved_k")
                sp.wait_ge(A["proj_lo"], UNITS * t + 8)
                for o in range(2):
                    half = slice(o * DH, (o + 1) * DH)
                    move(qs[0:DH, o::2, :], nat[half, 1, 0, :, :], "moved_q")
                    move(qs[DH:P, o::2, :], nat[half, 1, 1, :, :], "moved_q")
                    move(qm[0:DH, o::2, :], nat[half, 1, 0, :, :], "moved_q")
                if ts < ATILES - 1:
                    sp.wait_ge(A["proj_mm"], UNITS * t + UNITS)
                    load_h(t + 1)
                if ts > 0:
                    for j in range(2):
                        sp.wait_ge(A["fin_done"], 2 * (t - 1) + j + 1)
                        sp.dma_start(out_blk[2 * (t - 1) + j], res[:, j, :]).then_inc(out_stored[j], 16)

            sp.wait_ge(A["phase"], 5)
            load_h(0)
            sp.dma_start(bias_k[:, :, :], bk_dram.rearrange("h p c -> p h c")).then_inc(A["bias_k_loaded"], 16)
            sp.dma_start(fgain[:, :], final_gain.rearrange("(a d) -> a d", a=1).to_broadcast([P, D])).then_inc(A["fg_loaded"], 16)
            a_tiles(sp, tile)
            last = ATILES - 1
            for j in range(2):
                sp.wait_ge(out_stored[j], 16 * last)
                sp.dma_start(res[:, j, :], r_dram[2 * last + j]).then_inc(res_loaded[j], 16)
            for j in range(2):
                sp.wait_ge(A["fin_done"], 2 * last + j + 1)
                sp.dma_start(out_blk[2 * last + j], res[:, j, :]).then_inc(out_stored[j], 16)
            for j in range(2):
                sp.wait_ge(out_stored[j], 16 * ATILES)

        block = ctx.enter_context(nc.Block())

        @block.tensor
        def _(pe):
            p_phase_pe(pe)
            pe.nop().then_inc(A["phase"], 1)
            a_phase_pe(pe)

        @block.scalar
        def _(act):
            p_phase_act(act)
            act.wait_ge(S["yh_done"], GROUPS * PTILES)
            act.nop().then_inc(A["phase"], 1)
            a_phase_act(act)

        @block.vector
        def _(dve):
            p_phase_dve(dve)
            dve.wait_ge(S["r_done"], 2 * PBLK * PTILES)
            dve.nop().then_inc(A["phase"], 1)
            a_phase_dve(dve)

        @block.gpsimd
        def _(pool):
            p_phase_pool(pool)
            pool.wait_ge(S["yl_done"], GROUPS * PTILES)
            pool.nop().then_inc(A["phase"], 1)
            a_phase_pool(pool)

        @block.sync
        def _(sp):
            p_phase_sp(sp)
            sp.nop().then_inc(A["phase"], 1)
            a_phase_sp(sp)


def kernel(x, norm_gain, w_in, pool_w, pool_scale, rel_bias, w_out, final_norm_gain):
    import numpy as np
    import concourse.bacc as bacc
    from concourse.bass_utils import run_bass_kernel_spmd

    arrays = {
        "x": x, "norm_gain": norm_gain, "w_in": w_in, "pool_w": pool_w, "pool_scale": pool_scale,
        "rel_fwd": np.asarray(rel_bias)[0], "rel_rev": np.asarray(rel_bias)[0, :, ::-1],
        "w_out": w_out, "final_gain": final_norm_gain,
    }
    arrays = {f"in_{k}": np.ascontiguousarray(v) for k, v in arrays.items()}
    nc = bacc.Bacc("TRN2", target_bir_lowering=False, num_devices=1)
    args = [nc.dram_tensor(k, v.shape, mybir.dt.from_np(v.dtype), kind="ExternalInput").ap() for k, v in arrays.items()]
    args.append(nc.dram_tensor("out", (1, SEQ, D), F32, kind="ExternalOutput").ap())
    build(nc, *args)
    r = run_bass_kernel_spmd(nc, [arrays], core_ids=[0])
    return r.results[0]["out"]
```

```python
import math
from contextlib import ExitStack

import concourse.bass as bass
from concourse import mybir

F32 = mybir.dt.float32
F16 = mybir.dt.float16
BF16 = mybir.dt.bfloat16
ALU = mybir.AluOpType
ACT = mybir.ActivationFunctionType

P = 128
SEQ, D = 4096, 1024
KT = D // P
POOL, ATTN, DH, HEADS = 512, 512, 64, 8
WINDOWS = (2, 4, 8, 16)
GROUPS = len(WINDOWS)
CHUNK, MAX_REL = 64, 64
N_REL = 2 * MAX_REL + 1
EPS = 1e-6
NEG = -1e30

WS = 64.0
YS = 1.0 / 16
PS = 16.0

PT = 512
PTILES = SEQ // PT
PBLK = PT // P
HIST = 16
GORDER = (3, 2, 1, 0)

AT = 256
ATILES = SEQ // AT
RING = 6
NKT = ATTN // P
CHUNKS_LOOPED = 2
GROUP_BLOCKS = (((0, 0, 1), (1, 0, 2), (5, 1, 1)), ((2, 0, 2), (3, 0, 2)), ((4, 0, 2),))
GROUP_AT = (0, 512, 1024)
GROUP_BIAS = ((384, 128, 0), (256, 128, 128), (0, 256, 0))
EXT = 2 * P + 512


def at_least(eng, sem, n):
    if not isinstance(n, int) or n > 0:
        eng.wait_ge(sem, n)


def place(i, j):
    for g, blocks in enumerate(GROUP_BLOCKS):
        c = GROUP_AT[g]
        for bi, j0, n in blocks:
            if bi == i and j0 <= j < j0 + n:
                return c + (j - j0) * P
            c += n * P
    raise ValueError


def build(nc, x, norm_gain, w_in, pool_w, pool_scale, rel_fwd, rel_rev, w_out, final_gain, out):
    x_blk = x.rearrange("a (n p) d -> (a n) p d", p=P)
    out_blk = out.rearrange("a (n p) d -> (a n) p d", p=P)
    win_v = w_in[0].rearrange("(k p) n -> p k n", p=P)
    wout_v = w_out[0].rearrange("(k p) n -> k p n", p=P)
    h_dram = nc.dram_tensor("h_split", (ATILES, P, 2 * KT * AT), F16, kind="Internal").ap()
    r_dram = nc.dram_tensor("residual", (SEQ // P, P, D), F32, kind="Internal").ap()
    rel_dram = nc.dram_tensor("rel_rows", (2, HEADS, EXT), F32, kind="Internal").ap()
    bq_dram = nc.dram_tensor("bias_by_query", (HEADS, P, 640), F32, kind="Internal").ap()
    bk_dram = nc.dram_tensor("bias_by_key", (HEADS, P, 256), F32, kind="Internal").ap()

    ctx = ExitStack()
    with ctx:
        def sb(stack, name, shape, dt):
            return stack.enter_context(nc.sbuf_tensor(name, shape, dt))

        def sem(name):
            return ctx.enter_context(nc.semaphore(name))

        psum = [ctx.enter_context(nc.psum_tensor(f"bank{i}", [P, 512], F32)) for i in range(6)]
        wide = ctx.enter_context(nc.psum_tensor("bank67", [P, 1024], F32))

        ident = sb(ctx, "ident", [P, P], F32)
        ident16 = sb(ctx, "ident16", [P, P], F16)
        wa_h = sb(ctx, "wa_h", [P, 16, KT * P], F16)
        wa_l = sb(ctx, "wa_l", [P, 16, KT * P], F16)
        wob_h = sb(ctx, "wob_h", [P, NKT, D], F16)
        wob_l = sb(ctx, "wob_l", [P, NKT, D], F16)
        stat = sb(ctx, "stat", [P, 16], F32)
        pow_half = sb(ctx, "pow_half", [P, 1], F32)
        eps = sb(ctx, "eps", [P, 1], F32)

        pctx = ExitStack()
        wp_h = sb(pctx, "wp_h", [P, 8, KT * P], F16)
        wp_l = sb(pctx, "wp_l", [P, 8, KT * P], F16)
        wst = sb(pctx, "wst", [P, 2, KT, P], F32)
        xin = sb(pctx, "xin", [P, 2, D], F32)
        xn = sb(pctx, "xn", [P, D], F32)
        gain = sb(pctx, "gain", [P, D], F32)
        junk = sb(pctx, "junk", [P, D], BF16)
        hT = sb(pctx, "hT", [P, 2, KT, PT], F16)
        vb = sb(pctx, "vb", [P, 2, HIST + PT], F32)
        win = sb(pctx, "win", [P, 2, HIST + PT], F32)
        carry = sb(pctx, "carry", [P, GROUPS, HIST], F32)
        sig = sb(pctx, "sig", [P, PT], F32)
        inv_count = sb(pctx, "inv_count", [P, GROUPS, HIST], F32)
        psc = sb(pctx, "psc", [P, GROUPS], F32)
        rel = sb(pctx, "rel", [HEADS, 2, N_REL], F32)
        wot_h = sb(pctx, "wot_h", [P, NKT, D], F16)
        wot_l = sb(pctx, "wot_l", [P, NKT, D], F16)
        xres = sb(pctx, "xres", [P, 2, D], F32)
        yp_h = sb(pctx, "yp_h", [P, 2, NKT, PT], F16)
        yp_l = sb(pctx, "yp_l", [P, 2, NKT, PT], F16)
        pw = vb[:, 0, 0:PT].rearrange("p (g e) -> p g e", g=GROUPS)
        wvT = xres
        ext = yp_l[0:HEADS, :, :, :].rearrange("p a k n -> p (a k n)").bitcast(F32)[:, 0:2 * EXT].rearrange(
            "p (r u) -> p r u", r=2)

        names = """ident0 ident_ready id16 consts pw_loaded gain_loaded small_loaded ext_done ext_stored bias_stored psc_done
            w_hi w_lo fold_t fold_copied fold_mm
            ss_done ms_done rstd_done xn_done tr_done xth_done xtl_done h_stored
            v_mm g_mm vb_done sig_done z_done step_done y_done yh_done yl_done op_mm r_done
            phase_done""".split()
        S = {n: sem("p_" + n) for n in names}
        w_loaded = [sem(f"p_w_loaded{s}") for s in range(2)]
        start_loaded = [sem(f"p_start_loaded{n}") for n in range(2 * GROUPS + 2 * NKT)]
        x_loaded = [sem(f"p_x_loaded{s}") for s in range(2)]
        xres_loaded = [sem(f"p_xres_loaded{s}") for s in range(2)]
        r_stored = [sem(f"p_r_stored{s}") for s in range(2)]

        chunks = []
        for g in GORDER:
            chunks += [("v", g), ("g", g)]
        chunks += [("top", k) for k in range(NKT)] + [("bottom", k) for k in range(NKT)]
        STARTUP = len(chunks)

        def staged(n):
            whole = (wa_h if n < 8 else wa_l)[:, 2 * (n % 8):2 * (n % 8) + 2, :]
            return whole.rearrange("p a n -> p (a n)").bitcast(F32)

        def steps_before(t, k):
            done = sum(3 + g + 1 for g in GORDER[:k])
            total = sum(3 + g + 1 for g in GORDER)
            if isinstance(t, int) and t == 0:
                return done + 2 * k
            return total * t + 2 * GROUPS + done

        pj = psum[0:4]
        tr = psum[4:6]
        op = [wide[:, 0:512], wide[:, 512:1024]]

        def p_phase_pe(pe):
            def fold_transposes(k):
                pe.wait_ge(start_loaded[2 * k], 16)
                if k == 0:
                    pe.wait_ge(S["ident_ready"], 1)
                at_least(pe, S["fold_copied"], 2 * k)
                for half in range(2):
                    for q in range(4):
                        c = 4 * half + q
                        mm = nc.tensor.transpose(op[half][:, q * P:(q + 1) * P], staged(2 * k)[:, c * P:(c + 1) * P],
                                                 ident[:, :])
                    mm.then_inc(S["fold_t"], 1)

            def fold_products(k, g):
                if k == 0:
                    pe.wait_ge(S["pw_loaded"], 16)
                pe.wait_ge(S["fold_copied"], 2 * k + 2)
                at_least(pe, S["w_lo"], 2 * k - 3)
                for half in range(2):
                    bank = pj[2 * (k % 2) + half]
                    for q in range(4):
                        c = 4 * half + q
                        mm = nc.tensor.matmul(bank[:, q * P:(q + 1) * P], wvT[:, k % 2, c * P:(c + 1) * P],
                                              pw[:, g, :], start=True, stop=True)
                    mm.then_inc(S["fold_mm"], 1)

            def transposes(t, b):
                n = PBLK * t + b
                pe.wait_ge(S["xn_done"], n + 1)
                for half in range(2):
                    if isinstance(n, int):
                        at_least(pe, S["xtl_done"], 2 * (n - 1) + half + 1)
                    else:
                        pe.wait_ge(S["xtl_done"], 2 * (n - 1) + half + 1)
                    for q in range(4):
                        c = 4 * half + q
                        mm = nc.tensor.transpose(tr[half][:, q * P:(q + 1) * P], xn[:, c * P:(c + 1) * P], ident[:, :])
                    mm.then_inc(S["tr_done"], 1)

            def project(t, more=True):
                pe.wait_ge(S["xtl_done"], 2 * PBLK * t + 2 * PBLK)
                for k, g in enumerate(GORDER):
                    for what in range(2):
                        bank = pj[(2 * k + what) % 4]
                        if isinstance(t, int) and t == 0 and k < 2:
                            pe.wait_ge(S["w_lo"], 2 * GROUPS - 2 + 2 * k)
                        elif what == 0:
                            if k == GROUPS - 1 and more:
                                transposes(t + 1, 0)
                            pe.wait_ge(S["vb_done"], GROUPS * t + k - 1)
                        else:
                            pe.wait_ge(S["z_done"], GROUPS * t + k - 1)
                        c = 4 * what + g
                        for kt in range(KT):
                            wh = wp_h[:, c, kt * P:(kt + 1) * P]
                            wl = wp_l[:, c, kt * P:(kt + 1) * P]
                            nc.tensor.matmul(bank[:, :], wh, hT[:, 0, kt, :], start=(kt == 0), stop=False)
                            nc.tensor.matmul(bank[:, :], wh, hT[:, 1, kt, :], start=False, stop=False)
                            mm = nc.tensor.matmul(bank[:, :], wl, hT[:, 0, kt, :], start=False, stop=(kt == KT - 1))
                        mm.then_inc(S["g_mm" if what else "v_mm"], 1)

            def output(t, ts, b):
                n = PBLK * t + b
                if b == 0:
                    pe.wait_ge(S["yl_done"], GROUPS * t + GROUPS)
                    if ts == 0:
                        pe.wait_ge(S["w_lo"], 2 * GROUPS + NKT)
                for n2 in range(2):
                    if b > 0 or (isinstance(t, int) and t == PTILES - 1):
                        pe.wait_ge(S["r_done"], 2 * n - 1 + n2)
                    for kt in range(NKT):
                        yh = yp_h[:, ts % 2, kt, b * P:(b + 1) * P]
                        yl = yp_l[:, ts % 2, kt, b * P:(b + 1) * P]
                        for part, w in ((yh, wot_h), (yh, wot_l), (yl, wot_h)):
                            mm = nc.tensor.matmul(op[n2], part, w[:, kt, n2 * 512:(n2 + 1) * 512],
                                                  start=(kt == 0 and w is wot_h and part is yh),
                                                  stop=(kt == NKT - 1 and part is yl))
                mm.then_inc(S["op_mm"], 1)

            for k, g in enumerate(GORDER):
                fold_transposes(k)
                transposes(0, k)
                fold_products(k, g)
            project(0)
            for b in range(1, PBLK):
                transposes(1, b)
            with pe.Fori(0, (PTILES - 2) // 2) as it:
                for u in range(2):
                    t = 2 * it + (1 + u)
                    project(t)
                    for b in range(PBLK):
                        if b > 0:
                            transposes(t + 1, b)
                        output(t - 1, u, b)
            last = PTILES - 1
            project(last, more=False)
            pe.wait_ge(S["g_mm"], GROUPS * PTILES)
            pe.nop().then_inc(A["inputs_used"], 1)
            for t in (last - 1, last):
                for b in range(PBLK):
                    output(t, t, b)
            pe.wait_ge(S["op_mm"], PBLK * PTILES)
            pe.nop().then_inc(A["phase"], 1)

        def p_phase_act(act):
            def copy_transposed(k):
                for half in range(2):
                    act.wait_ge(S["fold_t"], 2 * k + half + 1)
                    at_least(act, S["fold_mm"], 2 * (k - 1))
                    nc.scalar.activation(wvT[:, k % 2, half * 512:(half + 1) * 512], op[half],
                                         ACT.Copy).then_inc(S["fold_copied"], 1)

            def split_hi(n):
                kind, c = chunks[n]
                if kind == "v":
                    k = n // 2
                    for half in range(2):
                        act.wait_ge(S["fold_mm"], 2 * k + half + 1)
                        ins = nc.scalar.activation(wp_h[:, c, half * 512:(half + 1) * 512],
                                                   pj[2 * (k % 2) + half][:, :], ACT.Copy, scale=WS)
                    ins.then_inc(S["w_hi"], 1)
                    return
                act.wait_ge(start_loaded[n], 16)
                dst = {"g": lambda: wp_h[:, 4 + c, :], "top": lambda: wot_h[:, c, :],
                       "bottom": lambda: wob_h[:, c, :]}[kind]()
                nc.scalar.activation(dst, staged(n), ACT.Copy, scale=WS).then_inc(S["w_hi"], 1)

            def split_hi_looped(t, i):
                act.wait_ge(w_loaded[i], 16 * t + 16)
                nc.scalar.activation(wa_h[:, CHUNKS_LOOPED * t + i, :], wst[:, i, :, :].rearrange("p k n -> p (k n)"),
                                     ACT.Copy, scale=WS).then_inc(S["w_hi"], 1)

            def square(t, b):
                n = PBLK * t + b
                act.wait_ge(x_loaded[b % 2], 16 * (2 * t + b // 2 + 1))
                if isinstance(n, int):
                    at_least(act, S["ms_done"], n - 1)
                    at_least(act, S["ss_done"], n)
                else:
                    act.wait_ge(S["ms_done"], n - 1)
                    act.wait_ge(S["ss_done"], n)
                nc.scalar.activation(junk[:, :], xin[:, b % 2, :], ACT.Square, scale=D ** -0.5,
                                     accum_out=stat[:, b % 2:b % 2 + 1]).then_inc(S["ss_done"], 1)

            def h_hi(t, b):
                for half in range(2):
                    act.wait_ge(S["tr_done"], 2 * (PBLK * t + b) + half + 1)
                    if b == 0 and half == 0 and not (isinstance(t, int) and t == 0):
                        act.wait_ge(S["g_mm"], GROUPS * t)
                        act.wait_ge(S["h_stored"], 32 * t)
                    nc.scalar.activation(hT[:, 0, 4 * half:4 * half + 4, b * P:(b + 1) * P],
                                         tr[half][:, :].rearrange("p (k n) -> p k n", k=4),
                                         ACT.Copy).then_inc(S["xth_done"], 1)

            def value(t, k):
                m = GROUPS * t + k
                act.wait_ge(S["v_mm"], m + 1)
                if isinstance(m, int):
                    at_least(act, S["yl_done"], m - 1)
                    if m == 0:
                        act.wait_ge(S["fold_mm"], 2 * GROUPS)
                else:
                    act.wait_ge(S["yl_done"], m - 1)
                nc.scalar.activation(vb[:, k % 2, HIST:], pj[(2 * k) % 4][:, :], ACT.Copy,
                                     scale=1 / WS).then_inc(S["vb_done"], 1)
                act.wait_ge(S["g_mm"], m + 1)
                if not (isinstance(m, int) and m == 0):
                    act.wait_ge(S["y_done"], m)
                nc.scalar.activation(sig[:, :], pj[(2 * k + 1) % 4][:, :], ACT.Tanh,
                                     scale=0.5 / WS).then_inc(S["sig_done"], 1)

            def y_hi(t, ts, k):
                m = GROUPS * t + k
                act.wait_ge(S["y_done"], m + 1)
                nc.scalar.activation(yp_h[:, ts % 2, GORDER[k], :], vb[:, k % 2, HIST:],
                                     ACT.Copy).then_inc(S["yh_done"], 1)

            def tile(t, ts, more=True):
                value(t, 0)
                if more:
                    square(t + 1, 0)
                    square(t + 1, 1)
                value(t, 1)
                y_hi(t, ts, 0)
                split_hi_looped(t, 0)
                value(t, 2)
                y_hi(t, ts, 1)
                if more:
                    square(t + 1, 2)
                split_hi_looped(t, 1)
                value(t, 3)
                if more:
                    h_hi(t + 1, 0)
                y_hi(t, ts, 2)
                y_hi(t, ts, 3)
                if more:
                    square(t + 1, 3)
                    for b in range(1, PBLK):
                        h_hi(t + 1, b)

            square(0, 0)
            square(0, 1)
            for k in range(GROUPS):
                copy_transposed(k)
                h_hi(0, k)
                if k < 2:
                    square(0, 2 + k)
                split_hi(2 * k)
                split_hi(2 * k + 1)
            act.wait_ge(S["small_loaded"], 48)
            nc.scalar.activation(psc[:, :], psc[:, :], ACT.Copy, scale=YS * 0.5 / WS).then_inc(S["psc_done"], 1)
            for n in range(2 * GROUPS, STARTUP):
                split_hi(n)
            tile(0, 0)
            with act.Fori(0, (PTILES - 2) // 2) as it:
                for u in range(2):
                    tile(2 * it + (1 + u), 1 + u)
            tile(PTILES - 1, PTILES - 1, more=False)
            act.wait_ge(S["yh_done"], GROUPS * PTILES)
            act.nop().then_inc(A["inputs_used"], 1)

        def p_phase_dve(dve):
            def split_lo(n):
                kind, c = chunks[n]
                dve.wait_ge(S["w_hi"], n + 1)
                if kind == "v":
                    for half in range(2):
                        cols = slice(half * 512, (half + 1) * 512)
                        ins = nc.vector.scalar_tensor_tensor(
                            out=wp_l[:, c, cols], in0=pj[n % 4 + half][:, :], scalar=WS, in1=wp_h[:, c, cols],
                            op0=ALU.mult, op1=ALU.subtract)
                    ins.then_inc(S["w_lo"], 1)
                    return
                hi, lo = {"g": (wp_h, wp_l), "top": (wot_h, wot_l), "bottom": (wob_h, wob_l)}[kind]
                i = 4 + c if kind == "g" else c
                nc.vector.scalar_tensor_tensor(
                    out=lo[:, i, :], in0=staged(n), scalar=WS,
                    in1=hi[:, i, :], op0=ALU.mult, op1=ALU.subtract).then_inc(S["w_lo"], 1)

            def split_lo_looped(t, i):
                c = CHUNKS_LOOPED * t + i
                dve.wait_ge(S["w_hi"], STARTUP + 1 + c)
                nc.vector.scalar_tensor_tensor(
                    out=wa_l[:, c, :], in0=wst[:, i, :, :].rearrange("p k n -> p (k n)"), scalar=WS,
                    in1=wa_h[:, c, :], op0=ALU.mult, op1=ALU.subtract).then_inc(S["w_lo"], 1)

            def normalise(t, b):
                n = PBLK * t + b
                dve.wait_ge(S["rstd_done"], n + 1)
                if isinstance(n, int):
                    if n == 0:
                        dve.wait_ge(S["gain_loaded"], 16)
                    at_least(dve, S["tr_done"], 2 * n)
                else:
                    dve.wait_ge(S["tr_done"], 2 * n)
                nc.vector.scalar_tensor_tensor(
                    out=xn[:, :], in0=xin[:, b % 2, :], scalar=stat[:, 4 + b % 2:5 + b % 2],
                    in1=gain[:, :], op0=ALU.mult, op1=ALU.mult).then_inc(S["xn_done"], 1)

            def h_lo(t, b):
                for half in range(2):
                    dve.wait_ge(S["xth_done"], 2 * (PBLK * t + b) + half + 1)
                    nc.vector.tensor_tensor(
                        hT[:, 1, 4 * half:4 * half + 4, b * P:(b + 1) * P],
                        tr[half][:, :].rearrange("p (k n) -> p k n", k=4),
                        hT[:, 0, 4 * half:4 * half + 4, b * P:(b + 1) * P],
                        ALU.subtract).then_inc(S["xtl_done"], 1)

            def pool(t, k):
                g = GORDER[k]
                w = WINDOWS[g]
                m = GROUPS * t + k
                first = isinstance(t, int) and t == 0
                step = [steps_before(t, k)]

                def link(ins):
                    ins.then_inc(S["step_done"], 1)
                    step[0] = step[0] + 1
                    return step[0]

                v = vb[:, k % 2, :]
                dve.wait_ge(S["sig_done"], m + 1)
                nc.vector.scalar_tensor_tensor(
                    out=sig[:, :], in0=sig[:, :], scalar=1.0, in1=pj[(2 * k + 1) % 4][:, :],
                    op0=ALU.add, op1=ALU.mult).then_inc(S["z_done"], 1)
                if first:
                    link(nc.vector.memset(v[:, 0:HIST], 0.0))
                else:
                    dve.wait_ge(S["step_done"], step[0])
                    link(nc.vector.tensor_copy(v[:, 0:HIST], carry[:, g, :]))
                dve.wait_ge(S["step_done"], step[0])
                dve.wait_ge(S["vb_done"], m + 1)
                link(nc.vector.tensor_copy(carry[:, g, :], v[:, PT:PT + HIST]))
                src, back = v, 1
                for level in range(g + 1):
                    dst = win[:, level % 2, :]
                    lo = 2 * back - 1
                    dve.wait_ge(S["step_done"], step[0])
                    link(nc.vector.tensor_tensor(dst[:, lo:], src[:, lo:], src[:, lo - back:HIST + PT - back], ALU.add))
                    src, back = dst, 2 * back
                other = win[:, (g + 1) % 2, 0:PT]
                dve.wait_ge(S["step_done"], step[0])
                link(nc.vector.scalar_tensor_tensor(
                    out=other, in0=src[:, HIST:], scalar=1.0 / w, in1=v[:, HIST:], op0=ALU.mult, op1=ALU.subtract))
                if first:
                    dve.wait_ge(S["step_done"], step[0])
                    dve.wait_ge(S["consts"], 3)
                    link(nc.vector.tensor_tensor(src[:, HIST:2 * HIST], src[:, HIST:2 * HIST], inv_count[:, g, :], ALU.mult))
                    dve.wait_ge(S["step_done"], step[0])
                    link(nc.vector.tensor_tensor(other[:, 0:HIST], src[:, HIST:2 * HIST], v[:, HIST:2 * HIST], ALU.subtract))
                dve.wait_ge(S["step_done"], step[0])
                dve.wait_ge(S["z_done"], m + 1)
                if first and k == 0:
                    dve.wait_ge(S["psc_done"], 1)
                nc.vector.scalar_tensor_tensor(
                    out=v[:, HIST:], in0=other, scalar=psc[:, g:g + 1], in1=sig[:, :],
                    op0=ALU.mult, op1=ALU.mult).then_inc(S["y_done"], 1)

            def residual(t, b):
                n = PBLK * t + b
                dve.wait_ge(S["op_mm"], n + 1)
                dve.wait_ge(xres_loaded[b % 2], 16 * (2 * t + b // 2 + 1))
                for n2 in range(2):
                    cols = slice(n2 * 512, (n2 + 1) * 512)
                    nc.vector.scalar_tensor_tensor(
                        out=xres[:, b % 2, cols], in0=op[n2], scalar=1.0 / (WS * YS), in1=xres[:, b % 2, cols],
                        op0=ALU.mult, op1=ALU.add).then_inc(S["r_done"], 1)

            def tile(t, more=True, before=True):
                pool(t, 0)
                if more:
                    normalise(t + 1, 0)
                pool(t, 1)
                split_lo_looped(t, 0)
                pool(t, 2)
                split_lo_looped(t, 1)
                if more:
                    normalise(t + 1, 1)
                pool(t, 3)
                for b in range(PBLK):
                    if more:
                        h_lo(t + 1, b)
                        if 0 < b < PBLK - 1:
                            normalise(t + 1, b + 1)
                    if before:
                        residual(t - 1, b)

            normalise(0, 0)
            for k in range(GROUPS):
                h_lo(0, k)
                if k + 1 < PBLK:
                    normalise(0, k + 1)
                split_lo(2 * k)
                split_lo(2 * k + 1)
            dve.wait_ge(S["ident_ready"], 1)
            nc.vector.tensor_copy(ident16[:, :], ident[:, :]).then_inc(S["id16"], 1)
            dve.wait_ge(S["small_loaded"], 48)
            for r in range(2):
                below = EXT - P - MAX_REL - 1 if r == 0 else P - MAX_REL - 1
                far = rel[:, r, 0:1] if r == 0 else rel[:, r, N_REL - 1:N_REL]
                above = EXT - below - N_REL
                for cols, src in ((slice(0, below), rel[:, r, 0:1].to_broadcast([HEADS, below])),
                                  (slice(below, below + N_REL), rel[:, r, :]),
                                  (slice(below + N_REL, EXT), rel[:, r, N_REL - 1:N_REL].to_broadcast([HEADS, above]))):
                    nc.vector.tensor_scalar(ext[:, r, cols], src, far, None, ALU.subtract).then_inc(S["ext_done"], 1)
            for n in range(2 * GROUPS, STARTUP):
                split_lo(n)
            tile(0, before=False)
            with dve.Fori(0, PTILES - 2) as it:
                tile(it + 1)
            tile(PTILES - 1, more=False)
            dve.wait_ge(S["y_done"], GROUPS * PTILES)
            dve.nop().then_inc(A["inputs_used"], 1)
            for b in range(PBLK):
                residual(PTILES - 1, b)
            dve.wait_ge(S["r_done"], 2 * PBLK * PTILES)
            dve.nop().then_inc(A["phase"], 1)

        def p_phase_pool(pool):
            def rstd(t, b):
                n = PBLK * t + b
                s = b % 2
                pool.wait_ge(S["ss_done"], n + 1)
                if isinstance(n, int):
                    at_least(pool, S["xn_done"], n - 1)
                else:
                    pool.wait_ge(S["xn_done"], n - 1)
                nc.gpsimd.tensor_tensor(stat[:, 2 + s:3 + s], stat[:, s:s + 1], eps[:, :], ALU.add).then_inc(S["ms_done"], 1)
                pool.wait_ge(S["ms_done"], n + 1)
                nc.gpsimd.tensor_tensor(stat[:, 4 + s:5 + s], stat[:, 2 + s:3 + s], pow_half[:, :],
                                        ALU.pow).then_inc(S["rstd_done"], 1)

            def y_lo(t, ts, k):
                m = GROUPS * t + k
                pool.wait_ge(S["yh_done"], m + 1)
                if ts == 0 and k == 0:
                    pool.wait_ge(S["ext_stored"], 16)
                nc.gpsimd.tensor_tensor(yp_l[:, ts % 2, GORDER[k], :], vb[:, k % 2, HIST:],
                                        yp_h[:, ts % 2, GORDER[k], :], ALU.subtract).then_inc(S["yl_done"], 1)

            def tile(t, ts, more=True):
                if more:
                    rstd(t + 1, 0)
                    rstd(t + 1, 1)
                y_lo(t, ts, 0)
                y_lo(t, ts, 1)
                if more:
                    rstd(t + 1, 2)
                y_lo(t, ts, 2)
                y_lo(t, ts, 3)
                if more:
                    rstd(t + 1, 3)

            nc.gpsimd.memset(ident[:, :], 0.0).then_inc(S["ident0"], 1)
            pool.wait_ge(S["ident0"], 1)
            nc.gpsimd.affine_select(out=ident[:, :], in_=ident[:, :], compare_op=ALU.not_equal, fill=1.0,
                                    base=0, pattern=[[-1, P]], channel_multiplier=1).then_inc(S["ident_ready"], 1)
            nc.gpsimd.memset(pow_half[:, :], -0.5).then_inc(S["consts"], 1)
            nc.gpsimd.memset(eps[:, :], EPS).then_inc(S["consts"], 1)
            pool.wait_ge(S["consts"], 2)
            for g, w in enumerate(WINDOWS):
                for c in range(w - 1):
                    nc.gpsimd.memset(inv_count[:, g, c:c + 1], 1.0 / (c + 1))
                ins = nc.gpsimd.memset(inv_count[:, g, w - 1:], 1.0 / w)
            ins.then_inc(S["consts"], 1)
            for b in range(PBLK):
                rstd(0, b)
            tile(0, 0)
            with pool.Fori(0, (PTILES - 2) // 2) as it:
                for u in range(2):
                    tile(2 * it + (1 + u), 1 + u)
            tile(PTILES - 1, PTILES - 1, more=False)
            pool.wait_ge(S["yl_done"], GROUPS * PTILES)
            pool.nop().then_inc(A["inputs_used"], 1)

        def p_phase_sp(sp):
            def load_chunk(n):
                kind, c = chunks[n]
                dst = staged(n)
                if kind in ("top", "bottom"):
                    src = wout_v[c if kind == "top" else NKT + c]
                else:
                    c += 0 if kind == "v" else GROUPS
                    src = win_v[:, :, c * P:(c + 1) * P]
                    dst = dst.rearrange("p (k n) -> p k n", k=KT)
                sp.dma_start(dst, src).then_inc(start_loaded[n], 16)

            def load_chunk_looped(t, i):
                c = CHUNKS_LOOPED * t + i
                if not (isinstance(t, int) and t == 0):
                    sp.wait_ge(S["w_lo"], STARTUP + c - 1)
                start = (c + 2 * GROUPS) * P
                src = win_v[:, :, bass.ds(start, P)]
                sp.dma_start(wst[:, i, :, :], src).then_inc(w_loaded[i], 16)

            def load_x(t, b):
                n = PBLK * t + b
                if isinstance(n, int):
                    at_least(sp, S["xn_done"], n - 1)
                else:
                    sp.wait_ge(S["xn_done"], n - 1)
                sp.dma_start(xin[:, b % 2, :], x_blk[n]).then_inc(x_loaded[b % 2], 16)

            def load_res(t, b):
                n = PBLK * t + b
                if isinstance(n, int) and n < 2:
                    sp.wait_ge(S["fold_mm"], 2 * GROUPS)
                else:
                    sp.wait_ge(r_stored[b % 2], 16 * (2 * t + b // 2))
                sp.dma_start(xres[:, b % 2, :], x_blk[n]).then_inc(xres_loaded[b % 2], 16)

            def store_res(t, b):
                n = PBLK * t + b
                sp.wait_ge(S["r_done"], 2 * n + 2)
                sp.dma_start(r_dram[n], xres[:, b % 2, :]).then_inc(r_stored[b % 2], 16)

            def store_h(t):
                sp.wait_ge(S["xtl_done"], 2 * PBLK * t + 2 * PBLK)
                for half in range(2):
                    sp.dma_start(h_dram[2 * t + half].rearrange("p (a n) -> p a n", a=2 * KT),
                                 hT[:, :, :, half * AT:(half + 1) * AT].rearrange("p s k n -> p (s k) n")
                                 ).then_inc(S["h_stored"], 16)

            def stores(t, more=True):
                for b in range(PBLK):
                    store_res(t, b)
                    if more or b < 2:
                        load_res(t if b < 2 else t + 1, (b + 2) % PBLK)

            def tile(t, more=True, before=True):
                if more:
                    load_x(t + 1, 0)
                    load_x(t + 1, 1)
                for i in range(CHUNKS_LOOPED):
                    load_chunk_looped(t, i)
                if more:
                    load_x(t + 1, 2)
                    load_x(t + 1, 3)
                if before:
                    stores(t - 1)
                if more:
                    store_h(t + 1)

            load_x(0, 0)
            load_chunk(0)
            sp.dma_start(gain[:, :], norm_gain[0:1, :].to_broadcast([P, D])).then_inc(S["gain_loaded"], 16)
            sp.dma_start(pw[:, :, :], pool_w[0].rearrange("g c e -> c g e")).then_inc(S["pw_loaded"], 16)
            load_x(0, 1)
            for n in range(1, 2 * GROUPS):
                load_chunk(n)
            load_x(0, 2)
            load_x(0, 3)
            sp.dma_start(psc[:, :], pool_scale[0].rearrange("(g p) -> p g", p=P),
                         allow_slow_non_contiguous=True).then_inc(S["small_loaded"], 16)
            sp.dma_start(rel[:, 0, :], rel_fwd).then_inc(S["small_loaded"], 16)
            sp.dma_start(rel[:, 1, :], rel_rev).then_inc(S["small_loaded"], 16)
            for n in range(2 * GROUPS, STARTUP):
                load_chunk(n)
            load_res(0, 0)
            load_res(0, 1)
            sp.wait_ge(S["ext_done"], 6)
            sp.dma_start(rel_dram.rearrange("r h u -> h r u"), ext[:, :, :]).then_inc(S["ext_stored"], 16)
            store_h(0)
            sp.wait_ge(S["ext_stored"], 16)
            for r, (dst, width) in enumerate(((bq_dram, 640), (bk_dram, 256))):
                sp.dma_start(dst, bass.AP(rel_dram.tensor, r * HEADS * EXT + P - 1, [[EXT, HEADS], [-1, P], [1, width]])
                             ).then_inc(S["bias_stored"], 16)
            tile(0, before=False)
            with sp.Fori(0, PTILES - 2) as it:
                tile(it + 1)
            tile(PTILES - 1, more=False)
            sp.wait_ge(S["bias_stored"], 32)
            sp.wait_ge(S["h_stored"], 32 * PTILES)
            sp.nop().then_inc(A["inputs_used"], 1)
            sp.wait_ge(A["inputs_used"], 5)
            sp.dma_start(hT2[:, :, :, :].rearrange("p s k n -> p (s k n)"), h_dram[0]).then_inc(A["h_loaded"], 16)
            stores(PTILES - 1, more=False)
            for s in range(2):
                sp.wait_ge(r_stored[s], 16 * 2 * PTILES)
            sp.nop().then_inc(A["phase"], 1)

        pctx.close()

        actx = ctx
        hT2 = sb(actx, "hT2", [P, 2, KT, AT], F16)
        nat = sb(actx, "nat", [P, 2, 2, 4, AT], F16)
        qs = sb(actx, "qs", [P, HEADS, AT], F16)
        qm = sb(actx, "qm", [DH + 1, HEADS, AT], F16)
        ks = sb(actx, "ks", [P, HEADS, RING * P], F16)
        kl = sb(actx, "kl", [DH + 1, HEADS, RING * P], F16)
        v_h = sb(actx, "v_h", [P, RING, HEADS, DH + 1], F16)
        v_l = sb(actx, "v_l", [P, RING, HEADS, DH], F16)
        sig2 = sb(actx, "sig2", [P, ATTN], F32)
        gate = sb(actx, "gate", [P, 2, ATTN], F32)
        p32 = sb(actx, "p32", [P, 2, 512], F32)
        p_h = sb(actx, "p_h", [P, 2, 1280], F16)
        p_l = sb(actx, "p_l", [P, 2, 1280], F16)
        bias_q = sb(actx, "bias_q", [P, HEADS, 640], BF16)
        bias_k = sb(actx, "bias_k", [P, HEADS, 256], F32)
        junk2 = sb(actx, "junk2", [P, 640], BF16)
        mx = sb(actx, "mx", [P, 2, 2], F32)
        m16 = sb(actx, "m16", [P, 2, 2], F16)
        rc = sb(actx, "rc", [P, 2, 2], F32)
        y = sb(actx, "y", [P, 2, ATTN], F32)
        yT_h = sb(actx, "yT_h", [P, NKT, AT], F16)
        yT_l = sb(actx, "yT_l", [P, NKT, AT], F16)
        res = sb(actx, "res", [P, 2, D], F32)
        fgain = sb(actx, "fgain", [P, D], F32)
        edge = sb(actx, "edge", [1, P + CHUNK], BF16)

        names = """inputs_used phase v_ones k_ones edge bias_q_loaded bias_k_loaded mask_done fg_loaded h_loaded
            proj_mm proj_hi proj_lo moved_k moved_q
            max_mm max_begun max_done m16_done mrow_mm mrow_done st_mm bias_done exp_done ph_done pl_done
            pv_mm rc_done ya_done yt_mm yth_done ytl_done op_mm res_done ss_done ms_done rstd_done fin_done""".split()
        A = {n: sem("a_" + n) for n in names}
        res_loaded = [sem(f"a_res_loaded{s}") for s in range(2)]
        out_stored = [sem(f"a_out_stored{s}") for s in range(2)]

        pja = psum[0:2]
        sta = psum[2:4]
        pva = psum[4]
        tra = psum[5]
        UNITS = 12
        KSCALE, QSCALE = 1 / WS, 1 / (WS * math.sqrt(DH))
        YSCALE = YS * 0.5 / WS

        def ring(ts, i):
            return (2 * ts - 4 + i) % RING

        def first_block(ts):
            return max(0, 4 - 2 * ts)

        def groups(ts):
            found = []
            for g, blocks in enumerate(GROUP_BLOCKS):
                have = [b for b in blocks if b[0] >= first_block(ts)]
                if have:
                    found.append((g, have))
            return found

        def seq(t, ts, h, k):
            n = len(groups(ts))
            if ts == 0:
                return n * h + k
            return HEADS * 3 * t - HEADS + n * h + k

        def span(g, have):
            cols = [(place(i, j0) - GROUP_AT[g], n * P) for i, j0, n in have]
            return cols[0][0], cols[-1][0] + cols[-1][1]

        def a_tiles(eng, tile):
            first = 3
            for t in range(first):
                tile(t, t)
            looped = (ATILES - first) // 3
            with eng.Fori(0, looped) as it:
                for u in range(3):
                    tile(3 * it + (first + u), first + u)
            for t in range(first + 3 * looped, ATILES):
                tile(t, t)

        def a_phase_pe(pe):
            def project(t, ts):
                pe.wait_ge(A["h_loaded"], 16 * t + 16)
                for u in range(UNITS):
                    bank = pja[u % 2]
                    if u < 2:
                        if ts >= 2:
                            pe.wait_ge(A["res_done"], 4 * (t - 1) - 1 + u)
                        elif ts == 1:
                            pe.wait_ge(A["proj_lo"], UNITS)
                    else:
                        pe.wait_ge(A["proj_lo"], UNITS * t + u - 1)
                    if u < 8:
                        c = (u + 4) % 8
                        for kt in range(KT):
                            wh = wa_h[:, c, kt * P:(kt + 1) * P]
                            wl = wa_l[:, c, kt * P:(kt + 1) * P]
                            nc.tensor.matmul(bank[:, 0:AT], wh, hT2[:, 0, kt, :], start=(kt == 0), stop=False)
                            nc.tensor.matmul(bank[:, 0:AT], wh, hT2[:, 1, kt, :], start=False, stop=False)
                            mm = nc.tensor.matmul(bank[:, 0:AT], wl, hT2[:, 0, kt, :], start=False, stop=(kt == KT - 1))
                    else:
                        j, c = (u - 8) // 2, 8 + 4 * (u % 2)
                        for kt in range(KT):
                            hh = hT2[:, 0, kt, j * P:(j + 1) * P]
                            hl = hT2[:, 1, kt, j * P:(j + 1) * P]
                            wh = wa_h[:, c:c + 4, kt * P:(kt + 1) * P]
                            wl = wa_l[:, c:c + 4, kt * P:(kt + 1) * P]
                            dst = bank[:, :].rearrange("p (c n) -> p c n", c=4)
                            nc.tensor.matmul(dst, hh, wh, start=(kt == 0), stop=False)
                            nc.tensor.matmul(dst, hh, wl, start=False, stop=False)
                            mm = nc.tensor.matmul(dst, hl, wh, start=False, stop=(kt == KT - 1))
                            if u == UNITS - 1 and kt == 4:
                                max_rows(t, ts, 0)
                    mm.then_inc(A["proj_mm"], 1)
                    if ts > 0 and u == 0:
                        values(t - 1, ts - 1, HEADS - 1)
                    if ts > 0 and u in (2, 4):
                        branch_transposes(t - 1, u // 2 - 1)
                    if u in (9, 10):
                        maxima(t, ts, 0, u - 9)

            def maxima(t, ts, h, j):
                if ts == 0 and h == 0 and j == 0:
                    pe.wait_ge(A["phase"], 3)
                    pe.wait_ge(A["edge"], 3)
                    pe.wait_ge(A["v_ones"], 1)
                    pe.wait_ge(A["k_ones"], 1)
                if h == 0 and j == 0:
                    pe.wait_ge(A["moved_k"], 96 * t + 96)
                    pe.wait_ge(A["moved_q"], 96 * t + 96)
                n = 2 * HEADS * t + 2 * h + j
                if not (ts == 0 and h == 0 and j == 0):
                    pe.wait_ge(A["max_done"], n)
                if ts > 0 and h == 0 and j == 0:
                    pe.wait_ge(A["ytl_done"], 2 * t)
                c = max(0, first_block(ts) - j) * P
                while c < 640:
                    i = j + c // P
                    run = 1
                    while (c + run * P < 640 and (c + run * P) % 512 and ring(ts, i + run) == ring(ts, i) + run):
                        run += 1
                    r = ring(ts, i)
                    mm = nc.tensor.matmul(wide[:, c:c + run * P], qs[0:DH, h, j * P:(j + 1) * P],
                                          ks[0:DH, h, r * P:(r + run) * P], start=True, stop=True)
                    c += run * P
                mm.then_inc(A["max_mm"], 1)

            def max_rows(t, ts, h):
                pe.wait_ge(A["m16_done"], HEADS * t + h + 1)
                if not (ts == 0 and h == 0):
                    pe.wait_ge(A["mrow_done"], HEADS * t + h)
                if h == 0 and ts > 0:
                    pe.wait_ge(A["ytl_done"], 2 * t)
                for j in range(2):
                    mm = nc.tensor.matmul(tra[DH:DH + 1, j * P:(j + 1) * P], m16[:, h % 2, j:j + 1], ident16[:, :],
                                          start=True, stop=True)
                mm.then_inc(A["mrow_mm"], 1)

            def scores(t, ts, h, k):
                g, have = groups(ts)[k]
                n = seq(t, ts, h, k)
                bank = sta[seq(ts, ts, h, k) % 2]
                if not (isinstance(n, int) and n < 2):
                    pe.wait_ge(A["exp_done"], n - 1)
                if k == 0:
                    pe.wait_ge(A["mrow_done"], HEADS * t + h + 1)
                for i, j0, w in have:
                    r = ring(ts, i)
                    c = place(i, j0) - GROUP_AT[g]
                    dst = bank[:, c:c + w * P]
                    qcols = slice(j0 * P, (j0 + w) * P)
                    masked = i < 2
                    nc.tensor.matmul(dst, ks[:, h, r * P:(r + 1) * P], qs[:, h, qcols], start=True, stop=False)
                    mm = nc.tensor.matmul(dst, kl[:, h, r * P:(r + 1) * P], qm[:, h, qcols], start=False, stop=not masked)
                    if masked:
                        m0 = c + (i - j0) * P + CHUNK
                        mm = nc.tensor.matmul(bank[:, m0:m0 + CHUNK], edge[:, 0:P], edge[:, P:P + CHUNK],
                                              start=False, stop=True)
                mm.then_inc(A["st_mm"], 1)

            def values(t, ts, h):
                n = seq(t, ts, h, len(groups(ts)))
                pe.wait_ge(A["pl_done"], n)
                if not (ts == 0 and h == 0):
                    pe.wait_ge(A["ya_done"], 2 * (HEADS * t + h))
                for j in range(2):
                    blocks = [i for i in range(j, j + 5) if i >= first_block(ts)]
                    acc = pva[:, j * (DH + 1):(j + 1) * (DH + 1)]
                    for i in blocks:
                        c, r = place(i, j), ring(ts, i)
                        ph, pl = p_h[:, h % 2, c:c + P], p_l[:, h % 2, c:c + P]
                        nc.tensor.matmul(acc, ph, v_h[:, r, h, :], start=(i == blocks[0]), stop=False)
                        nc.tensor.matmul(acc[:, 0:DH], ph, v_l[:, r, h, :], start=False, stop=False)
                        mm = nc.tensor.matmul(acc, pl, v_h[:, r, h, :], start=False, stop=(i == blocks[-1]))
                mm.then_inc(A["pv_mm"], 1)

            def branch_transposes(t, j):
                bank = tra if j == 0 else wide
                pe.wait_ge(A["ya_done"], 2 * HEADS * t + 2 * HEADS)
                for q in range(NKT):
                    mm = nc.tensor.transpose(bank[:, q * P:(q + 1) * P], y[:, j, q * P:(q + 1) * P], ident[:, :])
                mm.then_inc(A["yt_mm"], 1)

            def output(t, ts, h, low):
                j, kt = h // 4, h % 4
                if h == 0 and not low:
                    pe.wait_ge(A["ytl_done"], 2 * t + 2)
                yh, yl = yT_h[:, kt, j * P:(j + 1) * P], yT_l[:, kt, j * P:(j + 1) * P]
                if kt == 0 and not low and j == 0 and ts < ATILES - 1:
                    pe.wait_ge(A["proj_lo"], UNITS * t + 2 * UNITS)
                for n2 in range(2):
                    if kt == 0 and not low and (j > 0 or ts == ATILES - 1):
                        pe.wait_ge(A["res_done"], 4 * t + 2 * j - 1 + n2)
                    for part, w in ((yl, wob_h),) if low else ((yh, wob_h), (yh, wob_l)):
                        mm = nc.tensor.matmul(pja[n2][:, :], part, w[:, kt, n2 * 512:(n2 + 1) * 512],
                                              start=(kt == 0 and part is yh and w is wob_h),
                                              stop=(kt == NKT - 1 and part is yl))
                if kt == NKT - 1 and low:
                    mm.then_inc(A["op_mm"], 1)

            def tile(t, ts):
                project(t, ts)
                for h in range(HEADS):
                    if h + 1 < HEADS:
                        maxima(t, ts, h + 1, 0)
                    if ts > 0 and h > 0:
                        output(t - 1, ts - 1, h, False)
                    last = len(groups(ts)) - 1
                    for k in range(last + 1):
                        if k == last and h + 1 < HEADS:
                            maxima(t, ts, h + 1, 1)
                        if k == last and ts > 0 and h > 0:
                            output(t - 1, ts - 1, h, True)
                        scores(t, ts, h, k)
                    if ts > 0 and h == 0:
                        for low in (False, True):
                            output(t - 1, ts - 1, h, low)
                    if h > 0:
                        values(t, ts, h - 1)
                    if h + 1 < HEADS:
                        max_rows(t, ts, h + 1)

            pe.wait_ge(A["inputs_used"], 5)
            a_tiles(pe, tile)
            values(ATILES - 1, ATILES - 1, HEADS - 1)
            for j in range(2):
                branch_transposes(ATILES - 1, j)
            for h in range(HEADS):
                for low in (False, True):
                    output(ATILES - 1, ATILES - 1, h, low)

        def a_phase_act(act):
            def project_hi(t, ts):
                for u in range(UNITS):
                    if u == UNITS - 1:
                        max_row(t, ts, 0)
                    m = UNITS * t + u
                    act.wait_ge(A["proj_mm"], m + 1)
                    bank = pja[u % 2]
                    if u < 8:
                        which, pair = u // 4, u % 4
                        if pair == 0 and ts > 0:
                            act.wait_ge(A["moved_q" if which else "moved_k"], 96 * t)
                        ins = nc.scalar.activation(nat[:, which, 0, pair, :], bank[:, 0:AT], ACT.Copy,
                                                   scale=QSCALE if which else KSCALE)
                    else:
                        j = (u - 8) // 2
                        if u % 2 == 0:
                            r = ring(ts, 4 + j)
                            ins = nc.scalar.activation(v_h[:, r, :, 0:DH], bank[:, :].rearrange("p (h d) -> p h d", h=HEADS),
                                                       ACT.Copy, scale=1 / WS)
                        else:
                            act.wait_ge(A["proj_lo"], m - 1)
                            if u == 9 and ts >= 2:
                                act.wait_ge(A["ss_done"], 2 * (t - 1))
                            ins = nc.scalar.activation(sig2[:, :], bank[:, :], ACT.Tanh, scale=0.5 / WS)
                    ins.then_inc(A["proj_hi"], 1)
                    if ts > 0 and u in (2, 4):
                        branch_hi(t - 1, u // 2 - 1)

            def branch_hi(t, j):
                bank = tra if j == 0 else wide
                act.wait_ge(A["yt_mm"], 2 * t + j + 1)
                nc.scalar.activation(yT_h[:, :, j * P:(j + 1) * P],
                                     bank[:, 0:512].rearrange("p (k n) -> p k n", k=NKT),
                                     ACT.Copy, scale=YSCALE).then_inc(A["yth_done"], 1)

            def max_row(t, ts, h):
                act.wait_ge(A["mrow_mm"], HEADS * t + h + 1)
                nc.scalar.activation(qm[DH:DH + 1, h, :], tra[DH:DH + 1, 0:AT], ACT.Copy).then_inc(A["mrow_done"], 1)

            def exponentials(t, ts, h):
                for k, (g, have) in enumerate(groups(ts)):
                    n = seq(t, ts, h, k)
                    s = seq(ts, ts, h, k) % 2
                    a, b = span(g, have)
                    if k == len(groups(ts)) - 1 and h + 1 < HEADS:
                        max_row(t, ts, h + 1)
                    act.wait_ge(A["bias_done"], n + 1)
                    if not (isinstance(n, int) and n < 2):
                        act.wait_ge(A["pl_done"], n - 1)
                    nc.scalar.activation(p32[:, s, a:b], sta[s][:, a:b], ACT.Exp).then_inc(A["exp_done"], 1)
                    act.wait_ge(A["exp_done"], n + 1)
                    if k == 0 and not (ts == 0 and h < 2):
                        act.wait_ge(A["pv_mm"], HEADS * t + h - 1)
                    c = GROUP_AT[g]
                    nc.scalar.activation(p_h[:, h % 2, c + a:c + b], p32[:, s, a:b], ACT.Copy).then_inc(A["ph_done"], 1)

            def square(t, ts, j):
                n = 2 * t + j
                act.wait_ge(A["res_done"], 2 * n + 2)
                if not (ts == 0 and j == 0):
                    act.wait_ge(A["ss_done"], n)
                if ts > 0:
                    act.wait_ge(A["ms_done"], n - 1)
                nc.scalar.activation(sig2[:, :].bitcast(BF16), res[:, j, :], ACT.Square, scale=D ** -0.5,
                                     accum_out=stat[:, 8 + j:9 + j]).then_inc(A["ss_done"], 1)

            def tile(t, ts):
                project_hi(t, ts)
                for h in range(HEADS):
                    exponentials(t, ts, h)
                    if h == 4 and ts > 0:
                        square(t - 1, ts - 1, 0)
                if ts > 0:
                    square(t - 1, ts - 1, 1)

            act.wait_ge(A["inputs_used"], 5)
            a_tiles(act, tile)
            for j in range(2):
                branch_hi(ATILES - 1, j)
            for j in range(2):
                square(ATILES - 1, ATILES - 1, j)

        def a_phase_dve(dve):
            def project_lo(t, ts, u):
                m = UNITS * t + u
                dve.wait_ge(A["proj_hi"], m + 1)
                bank = pja[u % 2]
                if u < 8:
                    which, pair = u // 4, u % 4
                    ins = nc.vector.scalar_tensor_tensor(
                        out=nat[:, which, 1, pair, :], in0=bank[:, 0:AT], scalar=QSCALE if which else KSCALE,
                        in1=nat[:, which, 0, pair, :], op0=ALU.mult, op1=ALU.subtract)
                else:
                    j = (u - 8) // 2
                    if u % 2 == 0:
                        r = ring(ts, 4 + j)
                        ins = nc.vector.scalar_tensor_tensor(
                            out=v_l[:, r, :, :], in0=bank[:, :].rearrange("p (h d) -> p h d", h=HEADS), scalar=1 / WS,
                            in1=v_h[:, r, :, 0:DH], op0=ALU.mult, op1=ALU.subtract)
                    else:
                        ins = nc.vector.scalar_tensor_tensor(
                            out=gate[:, j, :], in0=sig2[:, :], scalar=1.0, in1=bank[:, :],
                            op0=ALU.add, op1=ALU.mult)
                ins.then_inc(A["proj_lo"], 1)
                if ts > 0 and u == 0:
                    attend(t - 1, ts - 1, HEADS - 1)
                if ts > 0 and u in (2, 4):
                    branch_lo(t - 1, u // 2 - 1)
                if ts > 1 and u == 3:
                    finish(t - 2, 1)
                if ts == 0 and u == 9:
                    mask_bias()
                if u in (9, 10):
                    maximum(t, ts, 0, u - 9)
                if u == 10:
                    minus_max(t, ts, 0)

            def branch_lo(t, j):
                bank = tra if j == 0 else wide
                dve.wait_ge(A["yth_done"], 2 * t + j + 1)
                nc.vector.scalar_tensor_tensor(
                    out=yT_l[:, :, j * P:(j + 1) * P], in0=bank[:, 0:512].rearrange("p (k n) -> p k n", k=NKT),
                    scalar=YSCALE, in1=yT_h[:, :, j * P:(j + 1) * P],
                    op0=ALU.mult, op1=ALU.subtract).then_inc(A["ytl_done"], 1)

            def mask_bias():
                dve.wait_ge(A["bias_q_loaded"], 16)
                dve.wait_ge(A["bias_k_loaded"], 16)
                dve.wait_ge(A["fg_loaded"], 16)
                nc.vector.memset(bias_q[CHUNK:P, :, 0:CHUNK], NEG).then_inc(A["mask_done"], 1)
                nc.vector.memset(bias_q[0:CHUNK, :, 640 - CHUNK:640], NEG).then_inc(A["mask_done"], 1)
                nc.vector.memset(bias_k[CHUNK:P, :, 0:CHUNK], NEG).then_inc(A["mask_done"], 1)
                dve.wait_ge(A["mask_done"], 3)

            def maximum(t, ts, h, j):
                n = 2 * HEADS * t + 2 * h + j
                c = max(0, first_block(ts) - j) * P
                dve.wait_ge(A["max_mm"], n + 1)
                if not (ts == 0 and h == 0 and j == 0):
                    dve.wait_ge(A["max_done"], n)
                if j == 0 and not (ts == 0 and h < 2):
                    dve.wait_ge(A["m16_done"], HEADS * t + h - 1)
                dve.sem_inc(A["max_begun"], 1)
                nc.vector.tensor_tensor_reduce(
                    junk2[:, c:640], wide[:, c:640], bias_q[:, h, c:640], 1.0, -3e38, ALU.add, ALU.max,
                    mx[:, h % 2, j:j + 1]).then_inc(A["max_done"], 1)

            def minus_max(t, ts, h):
                dve.wait_ge(A["max_done"], 2 * (HEADS * t + h + 1))
                if not (ts == 0 and h < 2):
                    dve.wait_ge(A["mrow_mm"], HEADS * t + h - 1)
                nc.vector.tensor_scalar(m16[:, h % 2, :], mx[:, h % 2, :], -1.0, math.log(PS),
                                        ALU.mult, ALU.add).then_inc(A["m16_done"], 1)

            def add_bias(t, ts, h, k):
                g, have = groups(ts)[k]
                n = seq(t, ts, h, k)
                bank = sta[seq(ts, ts, h, k) % 2]
                c, w, b = GROUP_BIAS[g]
                dve.wait_ge(A["st_mm"], n + 1)
                nc.vector.tensor_tensor(bank[:, c:c + w], bank[:, c:c + w], bias_k[:, h, b:b + w],
                                        ALU.add).then_inc(A["bias_done"], 1)

            def attend(t, ts, h):
                n = HEADS * t + h
                acc = pva[:, 0:2 * (DH + 1)].rearrange("p (j d) -> p j d", j=2)
                dve.wait_ge(A["pv_mm"], n + 1)
                if not (ts == 0 and h < 2):
                    dve.wait_ge(A["ya_done"], 2 * (n - 1))
                nc.vector.reciprocal(rc[:, h % 2, :], acc[:, :, DH]).then_inc(A["rc_done"], 1)
                dve.wait_ge(A["rc_done"], n + 1)
                if h == 0 and ts > 0:
                    dve.wait_ge(A["yt_mm"], 2 * t)
                for j in range(2):
                    nc.vector.scalar_tensor_tensor(
                        out=y[:, j, h * DH:(h + 1) * DH], in0=acc[:, j, 0:DH], scalar=rc[:, h % 2, j:j + 1],
                        in1=gate[:, j, h * DH:(h + 1) * DH], op0=ALU.mult, op1=ALU.mult).then_inc(A["ya_done"], 1)

            def residual(t, j, n2):
                n = 2 * t + j
                dve.wait_ge(A["op_mm"], n + 1)
                dve.wait_ge(res_loaded[j], 16 * t + 16)
                cols = slice(n2 * 512, (n2 + 1) * 512)
                nc.vector.scalar_tensor_tensor(
                    out=res[:, j, cols], in0=pja[n2][:, :], scalar=1.0 / (WS * YS), in1=res[:, j, cols],
                    op0=ALU.mult, op1=ALU.add).then_inc(A["res_done"], 1)

            def finish(t, j):
                n = 2 * t + j
                dve.wait_ge(A["rstd_done"], n + 1)
                nc.vector.scalar_tensor_tensor(
                    out=res[:, j, :], in0=res[:, j, :], scalar=stat[:, 12 + j:13 + j], in1=fgain[:, :],
                    op0=ALU.mult, op1=ALU.mult).then_inc(A["fin_done"], 1)

            def tile(t, ts):
                for u in range(UNITS - 1):
                    project_lo(t, ts, u)
                for h in range(HEADS):
                    if h + 1 < HEADS:
                        maximum(t, ts, h + 1, 0)
                    last = len(groups(ts)) - 1
                    for k in range(last + 1):
                        if h == 0 and k == last:
                            project_lo(t, ts, UNITS - 1)
                        if k == last and h + 1 < HEADS:
                            maximum(t, ts, h + 1, 1)
                            minus_max(t, ts, h + 1)
                        add_bias(t, ts, h, k)
                    if ts > 0 and h % 4 == 3:
                        for n2 in range(2):
                            residual(t - 1, h // 4, n2)
                    if h > 0:
                        attend(t, ts, h - 1)
                    if ts > 0 and h == 6:
                        finish(t - 1, 0)

            dve.wait_ge(A["inputs_used"], 5)
            nc.vector.memset(v_h[:, :, :, DH:DH + 1], 1.0).then_inc(A["v_ones"], 1)
            a_tiles(dve, tile)
            last = ATILES - 1
            attend(last, last, HEADS - 1)
            for j in range(2):
                branch_lo(last, j)
            finish(last - 1, 1)
            for j in range(2):
                for n2 in range(2):
                    residual(last, j, n2)
            for j in range(2):
                finish(last, j)

        def a_phase_pool(pool):
            def p_lo(t, ts, h):
                for k, (g, have) in enumerate(groups(ts)):
                    n = seq(t, ts, h, k)
                    s = seq(ts, ts, h, k) % 2
                    a, b = span(g, have)
                    c = GROUP_AT[g]
                    pool.wait_ge(A["ph_done"], n + 1)
                    nc.gpsimd.tensor_tensor(p_l[:, h % 2, c + a:c + b], p32[:, s, a:b], p_h[:, h % 2, c + a:c + b],
                                            ALU.subtract).then_inc(A["pl_done"], 1)

            def rstd(t, ts, j):
                n = 2 * t + j
                pool.wait_ge(A["ss_done"], n + 1)
                if ts > 0:
                    pool.wait_ge(A["fin_done"], n - 1)
                nc.gpsimd.tensor_tensor(stat[:, 10 + j:11 + j], stat[:, 8 + j:9 + j], eps[:, :], ALU.add).then_inc(A["ms_done"], 1)
                pool.wait_ge(A["ms_done"], n + 1)
                nc.gpsimd.tensor_tensor(stat[:, 12 + j:13 + j], stat[:, 10 + j:11 + j], pow_half[:, :],
                                        ALU.pow).then_inc(A["rstd_done"], 1)

            def tile(t, ts):
                for h in range(HEADS):
                    p_lo(t, ts, h)
                    if ts > 0 and h == 4:
                        rstd(t - 1, ts - 1, 0)
                if ts > 0:
                    rstd(t - 1, ts - 1, 1)

            pool.wait_ge(A["phase"], 3)
            nc.gpsimd.memset(kl[DH:DH + 1, :, :], 1.0).then_inc(A["k_ones"], 1)
            nc.gpsimd.memset(edge[:, 0:CHUNK], NEG).then_inc(A["edge"], 1)
            nc.gpsimd.memset(edge[:, CHUNK:P], 0.0).then_inc(A["edge"], 1)
            nc.gpsimd.memset(edge[:, P:], 1.0).then_inc(A["edge"], 1)
            pool.dma_start(bias_q[:, :, :], bq_dram.rearrange("h p c -> p h c")).then_inc(A["bias_q_loaded"], 16)
            a_tiles(pool, tile)
            for j in range(2):
                rstd(ATILES - 1, ATILES - 1, j)

        def a_phase_sp(sp):
            def load_h(t):
                sp.dma_start(hT2[:, :, :, :].rearrange("p s k n -> p (s k n)"), h_dram[t]).then_inc(A["h_loaded"], 16)

            def load_residual(t, ts, j):
                if ts > 0:
                    sp.wait_ge(out_stored[j], 16 * t)
                sp.dma_start(res[:, j, :], r_dram[2 * t + j]).then_inc(res_loaded[j], 16)

            def store(t, j):
                sp.wait_ge(A["fin_done"], 2 * t + j + 1)
                sp.dma_start(out_blk[2 * t + j], res[:, j, :]).then_inc(out_stored[j], 16)

            def move(dst, src, name):
                sp.dma_start(dst, src).then_inc(A[name], 16)

            def tile(t, ts):
                if ts > 0:
                    load_residual(t - 1, ts - 1, 0)
                r = ring(ts, 4) * P
                new = slice(r, r + AT)
                sp.wait_ge(A["proj_lo"], UNITS * t + 4)
                for o in range(2):
                    half = slice(o * DH, (o + 1) * DH)
                    for p0 in (0, DH):
                        move(ks[p0:p0 + DH, o::2, new], nat[half, 0, 0, :, :], "moved_k")
                    move(kl[0:DH, o::2, new], nat[half, 0, 1, :, :], "moved_k")
                if ts > 1:
                    store(t - 2, 1)
                sp.wait_ge(A["proj_lo"], UNITS * t + 8)
                for o in range(2):
                    half = slice(o * DH, (o + 1) * DH)
                    move(qs[0:DH, o::2, :], nat[half, 1, 0, :, :], "moved_q")
                    move(qs[DH:P, o::2, :], nat[half, 1, 1, :, :], "moved_q")
                    move(qm[0:DH, o::2, :], nat[half, 1, 0, :, :], "moved_q")
                if ts > 0:
                    load_residual(t - 1, ts - 1, 1)
                if ts < ATILES - 1:
                    sp.wait_ge(A["proj_mm"], UNITS * t + UNITS)
                    load_h(t + 1)
                if ts > 0:
                    store(t - 1, 0)

            sp.wait_ge(A["phase"], 3)
            sp.dma_start(bias_k[:, :, :], bk_dram.rearrange("h p c -> p h c")).then_inc(A["bias_k_loaded"], 16)
            sp.dma_start(fgain[:, :], final_gain.rearrange("(a d) -> a d", a=1).to_broadcast([P, D])).then_inc(A["fg_loaded"], 16)
            a_tiles(sp, tile)
            last = ATILES - 1
            load_residual(last, last, 0)
            store(last - 1, 1)
            load_residual(last, last, 1)
            for j in range(2):
                store(last, j)
            for j in range(2):
                sp.wait_ge(out_stored[j], 16 * ATILES)

        block = ctx.enter_context(nc.Block())

        @block.tensor
        def _(pe):
            p_phase_pe(pe)
            a_phase_pe(pe)

        @block.scalar
        def _(act):
            p_phase_act(act)
            a_phase_act(act)

        @block.vector
        def _(dve):
            p_phase_dve(dve)
            a_phase_dve(dve)

        @block.gpsimd
        def _(pool):
            p_phase_pool(pool)
            a_phase_pool(pool)

        @block.sync
        def _(sp):
            p_phase_sp(sp)
            a_phase_sp(sp)


def kernel(x, norm_gain, w_in, pool_w, pool_scale, rel_bias, w_out, final_norm_gain):
    import numpy as np
    import concourse.bacc as bacc
    from concourse.bass_utils import run_bass_kernel_spmd

    arrays = {
        "x": x, "norm_gain": norm_gain, "w_in": w_in, "pool_w": pool_w, "pool_scale": pool_scale,
        "rel_fwd": np.asarray(rel_bias)[0], "rel_rev": np.asarray(rel_bias)[0, :, ::-1],
        "w_out": w_out, "final_gain": final_norm_gain,
    }
    arrays = {f"in_{k}": np.ascontiguousarray(v) for k, v in arrays.items()}
    nc = bacc.Bacc("TRN2", target_bir_lowering=False, num_devices=1)
    args = [nc.dram_tensor(k, v.shape, mybir.dt.from_np(v.dtype), kind="ExternalInput").ap() for k, v in arrays.items()]
    args.append(nc.dram_tensor("out", (1, SEQ, D), F32, kind="ExternalOutput").ap())
    build(nc, *args)
    r = run_bass_kernel_spmd(nc, [arrays], core_ids=[0])
    return r.results[0]["out"]
```
